# Optimizing a Trainium2 kernel written in Bass

```python
import jax, jax.numpy as jnp
from jax import lax
import numpy as np
import math
import jax
import jax.numpy as jnp

D_MODEL = 1024
BATCH = 1
SEQ = 256
DEPTH = 2

BRANCH_WIDTH = D_MODEL // 2
N_BRANCHES = 4
ATT_HEADS = 8
ATT_KV_HEADS = 2
ATT_HEAD_DIM = BRANCH_WIDTH // ATT_HEADS
ROT_DIM = ATT_HEAD_DIM // 4
ROPE_THETA = 500000.0
IDX_HEADS = 4
IDX_HEAD_DIM = 64
INDEX_TOPK = 256
Q_BLOCK = 128
RWKV_HEAD = 64
RWKV_HEADS = BRANCH_WIDTH // RWKV_HEAD
RWKV_DECAY_LORA = 32
RWKV_A_LORA = 32
RWKV_GATE_LORA = 96
RWKV_GN_EPS = 64e-5
POOL_WINDOWS = (2, 4, 8, 16)
POOL_GROUPS = len(POOL_WINDOWS)
POOL_GROUP_DIM = BRANCH_WIDTH // POOL_GROUPS
RET_HEADS = 8
RET_KEY_DIM = BRANCH_WIDTH // 2 // RET_HEADS
RET_VALUE_DIM = BRANCH_WIDTH // RET_HEADS
RET_CHUNK = 128
RET_THETA = 10000.0
RET_GN_EPS = 1e-6
D_FF = 4 * D_MODEL
NORM_EPS = 1e-5

A_COLS = (ATT_HEADS * ATT_HEAD_DIM, ATT_KV_HEADS * ATT_HEAD_DIM, ATT_KV_HEADS * ATT_HEAD_DIM,
          IDX_HEADS * IDX_HEAD_DIM, IDX_HEAD_DIM, IDX_HEADS)
B_COLS = (BRANCH_WIDTH, RWKV_DECAY_LORA, BRANCH_WIDTH, BRANCH_WIDTH, RWKV_A_LORA, RWKV_GATE_LORA)
C_COLS = (BRANCH_WIDTH,)
D_COLS = (RET_HEADS * RET_KEY_DIM, RET_HEADS * RET_KEY_DIM, RET_HEADS * RET_VALUE_DIM, BRANCH_WIDTH)
N_A = sum(A_COLS)
N_B = sum(B_COLS)
N_C = sum(C_COLS)
N_D = sum(D_COLS)
N_G = N_BRANCHES * D_MODEL
N_IN = N_A + N_B + N_C + N_D + N_G


def rms_norm(x, g):
    xf = x.astype(jnp.float32)
    y = xf * lax.rsqrt(jnp.mean(xf * xf, -1, keepdims=True) + NORM_EPS)
    return (y * g.astype(jnp.float32)).astype(x.dtype)

def split_cols(p, sizes):
    outs, off = [], 0
    for sz in sizes:
        outs.append(p[..., off:off + sz])
        off += sz
    return outs

def cos_sin(positions, inv_freq, dtype):
    ang = positions.astype(jnp.float32)[..., None] * inv_freq
    return jnp.cos(ang).astype(dtype)[:, :, None, :], jnp.sin(ang).astype(dtype)[:, :, None, :]

def rotate(x, cos, sin):
    half = x.shape[-1] // 2
    x1, x2 = x[..., :half], x[..., half:]
    return jnp.concatenate([x1 * cos - x2 * sin, x2 * cos + x1 * sin], -1)

def partial_rope(x, cos, sin):
    return jnp.concatenate([rotate(x[..., :ROT_DIM], cos, sin), x[..., ROT_DIM:]], -1)

def dsa_attention(q, k, v, q_idx, k_idx, w_idx):
    b, s = q.shape[0], q.shape[1]
    top_k = min(INDEX_TOPK, s // 4)
    rep = ATT_HEADS // ATT_KV_HEADS
    scale = ATT_HEAD_DIM ** -0.5
    key_pos = jnp.arange(s)
    gather = jax.vmap(lambda kb, ib: kb[ib])

    def one_block(i):
        start = i * Q_BLOCK
        qb = lax.dynamic_slice_in_dim(q, start, Q_BLOCK, axis=1)
        qib = lax.dynamic_slice_in_dim(q_idx, start, Q_BLOCK, axis=1)
        wib = lax.dynamic_slice_in_dim(w_idx, start, Q_BLOCK, axis=1)
        qpos = start + jnp.arange(Q_BLOCK)
        causal = key_pos[None, :] <= qpos[:, None]
        idx_s = jax.nn.relu(jnp.einsum('bqhd,bsd->bqhs', qib, k_idx))
        idx_s = jnp.einsum('bqhs,bqh->bqs', idx_s, wib).astype(jnp.float32)
        idx_s = jnp.where(causal[None], idx_s, -jnp.inf)
        _, sel = lax.top_k(idx_s, top_k)
        valid = sel <= qpos[None, :, None]
        kg = gather(k, sel)
        vg = gather(v, sel)
        qg = qb.reshape(b, Q_BLOCK, ATT_KV_HEADS, rep, ATT_HEAD_DIM)
        logits = jnp.einsum('bqgrd,bqkgd->bqgrk', qg, kg).astype(jnp.float32) * scale
        logits = jnp.where(valid[:, :, None, None, :], logits, -jnp.inf)
        p = jax.nn.softmax(logits, axis=-1).astype(v.dtype)
        o = jnp.einsum('bqgrk,bqkgd->bqgrd', p, vg)
        return o.reshape(b, Q_BLOCK, ATT_HEADS * ATT_HEAD_DIM)

    out = lax.map(one_block, jnp.arange(s // Q_BLOCK))
    return jnp.swapaxes(out, 0, 1).reshape(b, s, ATT_HEADS * ATT_HEAD_DIM)

def token_shift(p, mu):
    prev = jnp.pad(p, ((0, 0), (1, 0), (0, 0)))[:, :-1]
    return p + (prev - p) * mu

def rwkv7_time_mix(p, mu, w0, w2, a0, a2, g2, k_k, k_a, r_k, ln_g, ln_b):
    b, s, _ = p.shape
    f32 = jnp.float32
    p = token_shift(p, mu)
    r, wd, k, v, ad, gd = split_cols(p, B_COLS)
    w = -jax.nn.softplus(-(w0 + jnp.tanh(wd) @ w2)) - 0.5
    a = jax.nn.sigmoid(a0 + ad @ a2)
    g = jax.nn.sigmoid(gd) @ g2
    heads = lambda t: t.astype(f32).reshape(b, s, RWKV_HEADS, RWKV_HEAD)
    hv = lambda t: t.astype(f32).reshape(RWKV_HEADS, RWKV_HEAD)
    r, w, k, v, a = heads(r), heads(w), heads(k), heads(v), heads(a)
    kk = k * hv(k_k)
    kk = kk / jnp.maximum(jnp.sqrt(jnp.sum(kk * kk, -1, keepdims=True)), 1e-12)
    k = k * (1.0 + (a - 1.0) * hv(k_a))
    decay = jnp.exp(-jnp.exp(w))

    def step(state, inp):
        r_t, d_t, k_t, v_t, kk_t, b_t = inp
        sk = jnp.einsum('bhij,bhj->bhi', state, kk_t)
        state = (state * d_t[:, :, None, :] - sk[..., None] * b_t[:, :, None, :]
                 + v_t[..., None] * k_t[:, :, None, :])
        return state, jnp.einsum('bhij,bhj->bhi', state, r_t)

    tm = lambda t: jnp.swapaxes(t, 0, 1)
    state0 = jnp.zeros((b, RWKV_HEADS, RWKV_HEAD, RWKV_HEAD), f32)
    _, y = lax.scan(step, state0, (tm(r), tm(decay), tm(k), tm(v), tm(kk), tm(kk * a)))
    y = jnp.swapaxes(y, 0, 1)
    mean = jnp.mean(y, -1, keepdims=True)
    var = jnp.mean(jnp.square(y - mean), -1, keepdims=True)
    y = (y - mean) * lax.rsqrt(var + RWKV_GN_EPS) * hv(ln_g) + hv(ln_b)
    y = y + jnp.sum(r * k * hv(r_k), -1, keepdims=True) * v
    return y.reshape(b, s, BRANCH_WIDTH).astype(p.dtype) * g

def multiscale_pool(p, pool_w, pool_scale):
    b, s, _ = p.shape
    xf = p.astype(jnp.float32)
    csum = jnp.pad(jnp.cumsum(xf, axis=1), ((0, 0), (1, 0), (0, 0)))
    steps = jnp.arange(1, s + 1, dtype=jnp.float32)
    groups = []
    for gi, win in enumerate(POOL_WINDOWS):
        lo, hi = gi * POOL_GROUP_DIM, (gi + 1) * POOL_GROUP_DIM
        c = csum[:, :, lo:hi]
        lagged = jnp.pad(c, ((0, 0), (win, 0), (0, 0)))[:, 1:s + 1]
        mean = (c[:, 1:] - lagged) / jnp.minimum(steps, float(win))[None, :, None]
        groups.append(mean - xf[:, :, lo:hi])
    pooled = jnp.stack(groups, axis=2).astype(p.dtype)
    y = jnp.einsum('bsgc,gcd->bsgd', pooled, pool_w).reshape(b, s, BRANCH_WIDTH)
    return y * pool_scale

def retention(q, k, v, g, gn_g):
    b, s, h, dk = q.shape
    dv = v.shape[-1]
    f32 = jnp.float32
    nc = s // RET_CHUNK
    log_gamma = jnp.log(1.0 - 2.0 ** (-5.0 - jnp.arange(h, dtype=f32)))
    pos = jnp.arange(RET_CHUNK, dtype=f32)
    diff = pos[:, None] - pos[None, :]
    intra = jnp.where(diff >= 0, jnp.exp(jnp.maximum(diff, 0.0)[None] * log_gamma[:, None, None]), 0.0)
    q_decay = jnp.exp((pos + 1.0)[None, :] * log_gamma[:, None])
    k_decay = jnp.exp((RET_CHUNK - 1.0 - pos)[None, :] * log_gamma[:, None])
    c_decay = jnp.exp(RET_CHUNK * log_gamma)
    chunk = lambda t: t.astype(f32).reshape(b, nc, RET_CHUNK, h, t.shape[-1]).transpose(1, 0, 3, 2, 4)
    qc, kc, vc = chunk(q), chunk(k * dk ** -0.5), chunk(v)

    def step(state, inp):
        qj, kj, vj = inp
        sc = jnp.einsum('bhnd,bhmd->bhnm', qj, kj) * intra
        o = (jnp.einsum('bhnm,bhmv->bhnv', sc, vj)
             + jnp.einsum('bhnd,bhdv->bhnv', qj, state) * q_decay[..., None])
        state = state * c_decay[:, None, None] + jnp.einsum('bhmd,bhmv->bhdv', kj * k_decay[..., None], vj)
        return state, o

    _, o = lax.scan(step, jnp.zeros((b, h, dk, dv), f32), (qc, kc, vc))
    o = o.transpose(1, 0, 3, 2, 4).reshape(b, s, h, dv)
    mean = jnp.mean(o, -1, keepdims=True)
    var = jnp.mean(jnp.square(o - mean), -1, keepdims=True)
    o = ((o - mean) * lax.rsqrt(var + RET_GN_EPS)).reshape(b, s, h * dv) * gn_g.astype(f32)
    return jax.nn.silu(g) * o.astype(g.dtype)

def first_inputs(seed: int = 0) -> dict:
    key = jax.random.key(seed)
    ks = jax.random.split(key, 32)
    f32 = jnp.float32
    nrm = lambda kk, shape, sc: jax.random.normal(kk, shape, f32) * sc
    L, D, W = DEPTH, D_MODEL, BRANCH_WIDTH
    return {
        'x': nrm(ks[0], (BATCH, SEQ, D), 1.0),
        'positions': jnp.tile(jnp.arange(SEQ, dtype=jnp.int32)[None, :], (BATCH, 1)),
        'attn_norm_g': 1.0 + nrm(ks[1], (L, D), 0.05),
        'w_in': nrm(ks[2], (L, D, N_IN), D ** -0.5),
        'rwkv_mu': jax.random.uniform(ks[3], (L, N_B), f32, 0.2, 0.8),
        'rwkv_w0': jnp.linspace(-6.0, -1.0, W, dtype=f32)[None, :] + nrm(ks[4], (L, W), 0.1),
        'rwkv_w2': nrm(ks[5], (L, RWKV_DECAY_LORA, W), 0.5 * RWKV_DECAY_LORA ** -0.5),
        'rwkv_a0': nrm(ks[6], (L, W), 0.1),
        'rwkv_a2': nrm(ks[7], (L, RWKV_A_LORA, W), RWKV_A_LORA ** -0.5),
        'rwkv_g2': nrm(ks[8], (L, RWKV_GATE_LORA, W), RWKV_GATE_LORA ** -0.5),
        'rwkv_k_k': 0.85 + nrm(ks[9], (L, W), 0.05),
        'rwkv_k_a': 1.0 + nrm(ks[10], (L, W), 0.05),
        'rwkv_r_k': nrm(ks[11], (L, W), 0.1),
        'rwkv_ln_g': 1.0 + nrm(ks[12], (L, W), 0.05),
        'rwkv_ln_b': nrm(ks[13], (L, W), 0.05),
        'pool_w': nrm(ks[14], (L, POOL_GROUPS, POOL_GROUP_DIM, POOL_GROUP_DIM), POOL_GROUP_DIM ** -0.5),
        'pool_scale': 1.0 + nrm(ks[15], (L, W), 0.1),
        'ret_gn_g': 1.0 + nrm(ks[16], (L, W), 0.05),
        'gate_b': nrm(ks[17], (L, N_BRANCHES, D), 0.1),
        'w_branch': nrm(ks[18], (L, N_BRANCHES, W, D), W ** -0.5),
        'w_out': nrm(ks[19], (L, D, D), D ** -0.5),
        'mlp_norm_g': 1.0 + nrm(ks[20], (L, D), 0.05),
        'mlp_up': nrm(ks[21], (L, D, D_FF), D ** -0.5),
        'mlp_down': nrm(ks[22], (L, D_FF, D), D_FF ** -0.5),
        'final_norm_g': 1.0 + nrm(ks[23], (D,), 0.05),
    }

def first_block(x, positions, attn_norm_g, w_in, rwkv_mu, rwkv_w0, rwkv_w2, rwkv_a0, rwkv_a2, rwkv_g2,
              rwkv_k_k, rwkv_k_a, rwkv_r_k, rwkv_ln_g, rwkv_ln_b, pool_w, pool_scale, ret_gn_g,
              gate_b, w_branch, w_out, mlp_norm_g, mlp_up, mlp_down, final_norm_g):
    b, s, _ = x.shape
    dt = x.dtype
    inv_freq_att = ROPE_THETA ** (-jnp.arange(0, ROT_DIM, 2, dtype=jnp.float32) / ROT_DIM)
    cos_a, sin_a = cos_sin(positions, inv_freq_att, dt)
    inv_freq_ret = 1.0 / (RET_THETA ** jnp.linspace(0.0, 1.0, RET_KEY_DIM // 2, dtype=jnp.float32))
    cos_r, sin_r = cos_sin(positions, inv_freq_ret, dt)
    for l in range(DEPTH):
        h = rms_norm(x, attn_norm_g[l])
        proj = h @ w_in[l]
        pa, pb, pc, pd, pg = split_cols(proj, (N_A, N_B, N_C, N_D, N_G))
        q, k, v, qi, ki, wi = split_cols(pa, A_COLS)
        q = partial_rope(q.reshape(b, s, ATT_HEADS, ATT_HEAD_DIM), cos_a, sin_a)
        k = partial_rope(k.reshape(b, s, ATT_KV_HEADS, ATT_HEAD_DIM), cos_a, sin_a)
        v = v.reshape(b, s, ATT_KV_HEADS, ATT_HEAD_DIM)
        qi = partial_rope(qi.reshape(b, s, IDX_HEADS, IDX_HEAD_DIM), cos_a, sin_a)
        ki = partial_rope(ki[:, :, None, :], cos_a, sin_a)[:, :, 0]
        o_a = dsa_attention(q, k, v, qi, ki, wi)
        o_b = rwkv7_time_mix(pb, rwkv_mu[l], rwkv_w0[l], rwkv_w2[l], rwkv_a0[l], rwkv_a2[l], rwkv_g2[l],
                             rwkv_k_k[l], rwkv_k_a[l], rwkv_r_k[l], rwkv_ln_g[l], rwkv_ln_b[l])
        o_c = multiscale_pool(pc, pool_w[l], pool_scale[l])
        rq, rk, rv, rg = split_cols(pd, D_COLS)
        rq = rotate(rq.reshape(b, s, RET_HEADS, RET_KEY_DIM), cos_r, sin_r)
        rk = rotate(rk.reshape(b, s, RET_HEADS, RET_KEY_DIM), cos_r, sin_r)
        o_d = retention(rq, rk, rv.reshape(b, s, RET_HEADS, RET_VALUE_DIM), rg, ret_gn_g[l])
        gates = jax.nn.sigmoid(pg.reshape(b, s, N_BRANCHES, D_MODEL) + gate_b[l])
        merged = gates[:, :, 0] * (o_a @ w_branch[l, 0])
        merged = merged + gates[:, :, 1] * (o_b @ w_branch[l, 1])
        merged = merged + gates[:, :, 2] * (o_c @ w_branch[l, 2])
        merged = merged + gates[:, :, 3] * (o_d @ w_branch[l, 3])
        x = x + merged @ w_out[l]
        h2 = rms_norm(x, mlp_norm_g[l])
        x = x + jnp.square(jax.nn.relu(h2 @ mlp_up[l])) @ mlp_down[l]
    return rms_norm(x, final_norm_g)


N_EVEN = (DEPTH + 1) // 2
N_ODD = DEPTH // 2
EPS = 1e-6
ROPE_THETA_2 = 10000.0

GDN_HEADS = 4
GDN_DK = 128
GDN_DV = 128
GDN_CONV = 4
GDN_CHUNK = 64
GDN_QK = GDN_HEADS * GDN_DK
GDN_V = GDN_HEADS * GDN_DV
GDN_CONV_CH = 2 * GDN_QK + GDN_V
MOBA_HEADS = 4
MOBA_DH = 128
MOBA_BLOCK = 256
MOBA_TOPK = 3
MOBA_W = MOBA_HEADS * MOBA_DH
HY_SIZES = (GDN_CONV_CH, GDN_V, GDN_HEADS, GDN_HEADS, MOBA_W, MOBA_W, MOBA_W)
HY_IN = sum(HY_SIZES)
HY_SPLITS = tuple(int(i) for i in np.cumsum(HY_SIZES)[:-1])
HY_OUT = GDN_V + MOBA_W
MLA_HEADS = 8
MLA_Q_RANK = 512
MLA_KV_RANK = 256
MLA_NOPE = 128
MLA_ROPE = 64
MLA_V = 128
MLA_IN = MLA_Q_RANK + MLA_KV_RANK + MLA_ROPE
PEER_HEADS = 8
PEER_NKEYS = 128
PEER_EXPERTS = PEER_NKEYS * PEER_NKEYS
PEER_DKEY = 256
PEER_TOPK = 16
PEER_TOK_CHUNK = 128


def rmsnorm(x, w):
    xf = x.astype(jnp.float32)
    y = xf * lax.rsqrt(jnp.mean(xf * xf, axis=-1, keepdims=True) + EPS)
    return (y * w.astype(jnp.float32)).astype(x.dtype)

def l2norm(x):
    xf = x.astype(jnp.float32)
    return xf * lax.rsqrt(jnp.sum(xf * xf, axis=-1, keepdims=True) + EPS)

def rope_tables(positions, dim):
    inv_freq = ROPE_THETA_2 ** (-jnp.arange(0, dim, 2, dtype=jnp.float32) / dim)
    ang = positions.astype(jnp.float32)[..., None] * inv_freq
    return jnp.cos(ang), jnp.sin(ang)

def apply_rope(x, cos, sin):
    x1, x2 = jnp.split(x.astype(jnp.float32), 2, axis=-1)
    c = cos[:, :, None, :]
    s = sin[:, :, None, :]
    return jnp.concatenate([x1 * c - x2 * s, x2 * c + x1 * s], axis=-1)

def causal_conv_silu(x, w):
    k_w = w.shape[0]
    s = x.shape[1]
    xp = jnp.pad(x, ((0, 0), (k_w - 1, 0), (0, 0)))
    y = xp[:, 0:s] * w[0]
    for j in range(1, k_w):
        y = y + xp[:, j:j + s] * w[j]
    return jax.nn.silu(y)

def unit_lower_inverse(l_strict):
    n = l_strict.shape[-1]
    eye = jnp.eye(n, dtype=l_strict.dtype)
    neg = -l_strict
    inv = eye + neg
    power = neg
    p = 2
    while p < n:
        power = power @ power
        inv = inv @ (eye + power)
        p *= 2
    return inv

def gated_delta_rule(q, k, v, g, beta):
    bsz, s, nh, dk = q.shape
    dv = v.shape[-1]
    cs = GDN_CHUNK
    nc = s // cs

    def to_chunks(t):
        t = t.reshape((bsz, nc, cs, nh) + t.shape[3:])
        return jnp.moveaxis(t, 3, 1)

    q = to_chunks(q * dk ** -0.5)
    k = to_chunks(k)
    v = to_chunks(v)
    beta = to_chunks(beta)
    g = jnp.cumsum(to_chunks(g), axis=-1)
    causal = jnp.tril(jnp.ones((cs, cs), dtype=bool))
    strict = jnp.tril(jnp.ones((cs, cs), dtype=bool), -1)
    decay = jnp.exp(jnp.where(causal, g[..., :, None] - g[..., None, :], -jnp.inf))
    k_beta = k * beta[..., None]
    l_strict = jnp.where(strict, jnp.einsum('bhncd,bhnmd->bhncm', k_beta, k) * decay, 0.0)
    t_inv = unit_lower_inverse(l_strict)
    u = t_inv @ (v * beta[..., None])
    w = t_inv @ (k_beta * jnp.exp(g)[..., None])
    qk = jnp.einsum('bhncd,bhnmd->bhncm', q, k) * decay
    q_dec = q * jnp.exp(g)[..., None]
    g_last = g[..., -1]
    k_dec = k * jnp.exp(g_last[..., None] - g)[..., None]

    def step(state, inp):
        qd, kd, uc, wc, qkc, gl = inp
        v_new = uc - jnp.einsum('bhck,bhkv->bhcv', wc, state)
        out = jnp.einsum('bhck,bhkv->bhcv', qd, state) + jnp.einsum('bhcm,bhmv->bhcv', qkc, v_new)
        state = state * jnp.exp(gl)[..., None, None] + jnp.einsum('bhck,bhcv->bhkv', kd, v_new)
        return state, out

    xs = tuple(jnp.moveaxis(t, 2, 0) for t in (q_dec, k_dec, u, w, qk, g_last))
    state0 = jnp.zeros((bsz, nh, dk, dv), jnp.float32)
    _, o = lax.scan(step, state0, xs)
    return jnp.transpose(o, (1, 0, 3, 2, 4)).reshape(bsz, s, nh, dv)

def moba_attention(q, k, v):
    bsz, s, nh, d = q.shape
    nb = -(-s // MOBA_BLOCK)
    pad = nb * MOBA_BLOCK - s
    topk = min(MOBA_TOPK, nb)
    qh = jnp.moveaxis(q, 2, 1) * d ** -0.5

    def to_blocks(t):
        t = jnp.pad(jnp.moveaxis(t, 2, 1), ((0, 0), (0, 0), (0, pad), (0, 0)))
        return t.reshape(bsz, nh, nb, MOBA_BLOCK, d)

    k_blk = to_blocks(k)
    v_blk = to_blocks(v)
    k_mean = jnp.mean(k_blk, axis=3)
    b_idx = jnp.arange(bsz)[:, None, None, None]
    h_idx = jnp.arange(nh)[None, :, None, None]
    blk_ids = jnp.arange(nb)

    def one_block(ci):
        start = ci * Q_BLOCK
        own = start // MOBA_BLOCK
        qc = lax.dynamic_slice_in_dim(qh, start, Q_BLOCK, axis=2)
        qpos = start + jnp.arange(Q_BLOCK)
        gate = jnp.einsum('bhqd,bhnd->bhqn', qc, k_mean)
        gate = jnp.where(blk_ids < own, gate, -jnp.inf)
        _, sel = lax.top_k(gate, topk)
        valid = sel < own
        k_sel = k_blk[b_idx, h_idx, sel]
        v_sel = v_blk[b_idx, h_idx, sel]
        s_sel = jnp.einsum('bhqd,bhqtkd->bhqtk', qc, k_sel)
        s_sel = jnp.where(valid[..., None], s_sel, -jnp.inf).reshape(bsz, nh, Q_BLOCK, topk * MOBA_BLOCK)
        k_own = lax.dynamic_index_in_dim(k_blk, own, axis=2, keepdims=False)
        v_own = lax.dynamic_index_in_dim(v_blk, own, axis=2, keepdims=False)
        kpos = own * MOBA_BLOCK + jnp.arange(MOBA_BLOCK)
        s_own = jnp.einsum('bhqd,bhkd->bhqk', qc, k_own)
        s_own = jnp.where(kpos[None, :] <= qpos[:, None], s_own, -jnp.inf)
        p = jax.nn.softmax(jnp.concatenate([s_sel, s_own], axis=-1), axis=-1)
        p_sel = p[..., :topk * MOBA_BLOCK].reshape(bsz, nh, Q_BLOCK, topk, MOBA_BLOCK)
        p_own = p[..., topk * MOBA_BLOCK:]
        return (jnp.einsum('bhqtk,bhqtkd->bhqd', p_sel, v_sel)
                + jnp.einsum('bhqk,bhkd->bhqd', p_own, v_own))

    o = lax.map(one_block, jnp.arange(s // Q_BLOCK))
    return jnp.transpose(o, (1, 0, 3, 2, 4)).reshape(bsz, s, nh, d)

def hybrid_mixer(h, cos, sin, w_in, conv_w, a_log, dt_bias, o_norm, w_out):
    bsz, s, _ = h.shape
    f32 = jnp.float32
    qkv_a, z_a, b_a, a_a, q_b, k_b, v_b = jnp.split(h @ w_in, HY_SPLITS, axis=-1)
    qkv_a = causal_conv_silu(qkv_a, conv_w)
    q_a, k_a, v_a = jnp.split(qkv_a, [GDN_QK, 2 * GDN_QK], axis=-1)
    q_a = l2norm(q_a.reshape(bsz, s, GDN_HEADS, GDN_DK))
    k_a = l2norm(k_a.reshape(bsz, s, GDN_HEADS, GDN_DK))
    v_a = v_a.reshape(bsz, s, GDN_HEADS, GDN_DV).astype(f32)
    beta = jax.nn.sigmoid(b_a.astype(f32))
    g = -jnp.exp(a_log.astype(f32)) * jax.nn.softplus(a_a.astype(f32) + dt_bias.astype(f32))
    o_a = gated_delta_rule(q_a, k_a, v_a, g, beta)
    o_a = rmsnorm(o_a, o_norm) * jax.nn.silu(z_a.reshape(bsz, s, GDN_HEADS, GDN_DV).astype(f32))
    q_b = apply_rope(q_b.reshape(bsz, s, MOBA_HEADS, MOBA_DH), cos, sin)
    k_b = apply_rope(k_b.reshape(bsz, s, MOBA_HEADS, MOBA_DH), cos, sin)
    v_b = v_b.reshape(bsz, s, MOBA_HEADS, MOBA_DH).astype(f32)
    o_b = moba_attention(q_b, k_b, v_b)
    o = jnp.concatenate([o_a.reshape(bsz, s, GDN_V), o_b.reshape(bsz, s, MOBA_W)], axis=-1)
    return o.astype(h.dtype) @ w_out

def mla_mixer(h, cos, sin, w_in, q_norm, kv_norm, w_uq, w_ukv, w_out):
    bsz, s, _ = h.shape
    f32 = jnp.float32
    cq, ckv, k_rope = jnp.split(h @ w_in, [MLA_Q_RANK, MLA_Q_RANK + MLA_KV_RANK], axis=-1)
    q = (rmsnorm(cq, q_norm) @ w_uq).reshape(bsz, s, MLA_HEADS, MLA_NOPE + MLA_ROPE)
    kv = (rmsnorm(ckv, kv_norm) @ w_ukv).reshape(bsz, s, MLA_HEADS, MLA_NOPE + MLA_V)
    q_nope, q_rope = jnp.split(q.astype(f32), [MLA_NOPE], axis=-1)
    k_nope, val = jnp.split(kv.astype(f32), [MLA_NOPE], axis=-1)
    q_rope = apply_rope(q_rope, cos, sin)
    k_rope = apply_rope(k_rope[:, :, None, :], cos, sin)[:, :, 0, :]
    scale = (MLA_NOPE + MLA_ROPE) ** -0.5
    qn = jnp.moveaxis(q_nope, 2, 1) * scale
    qr = jnp.moveaxis(q_rope, 2, 1) * scale
    kn = jnp.moveaxis(k_nope, 2, 1)
    vh = jnp.moveaxis(val, 2, 1)
    kpos = jnp.arange(s)

    def one_block(bi):
        start = bi * Q_BLOCK
        qn_b = lax.dynamic_slice_in_dim(qn, start, Q_BLOCK, axis=2)
        qr_b = lax.dynamic_slice_in_dim(qr, start, Q_BLOCK, axis=2)
        scores = (jnp.einsum('bhqd,bhkd->bhqk', qn_b, kn)
                  + jnp.einsum('bhqr,bkr->bhqk', qr_b, k_rope))
        qpos = start + jnp.arange(Q_BLOCK)
        scores = jnp.where(kpos[None, :] <= qpos[:, None], scores, -jnp.inf)
        return jnp.einsum('bhqk,bhkd->bhqd', jax.nn.softmax(scores, axis=-1), vh)

    o = lax.map(one_block, jnp.arange(s // Q_BLOCK))
    o = jnp.transpose(o, (1, 0, 3, 2, 4)).reshape(bsz, s, MLA_HEADS * MLA_V)
    return o.astype(h.dtype) @ w_out

def peer_ffn(h, w_q, sub_keys, u, v):
    bsz, s, d = h.shape
    f32 = jnp.float32
    q = (h @ w_q).astype(f32).reshape(bsz, s, PEER_HEADS, 2, PEER_DKEY // 2)
    scores = jnp.einsum('bshpd,hpnd->bshpn', q, sub_keys.astype(f32))
    s1, i1 = lax.top_k(scores[..., 0, :], PEER_TOPK)
    s2, i2 = lax.top_k(scores[..., 1, :], PEER_TOPK)
    n_cand = PEER_TOPK * PEER_TOPK
    cand = (s1[..., :, None] + s2[..., None, :]).reshape(bsz, s, PEER_HEADS, n_cand)
    cand_idx = (i1[..., :, None] * PEER_NKEYS + i2[..., None, :]).reshape(bsz, s, PEER_HEADS, n_cand)
    top, pos = lax.top_k(cand, PEER_TOPK)
    expert = jnp.take_along_axis(cand_idx, pos, axis=-1)
    gates = jax.nn.softmax(top, axis=-1)
    n_tok = bsz * s
    n_sel = PEER_HEADS * PEER_TOPK
    n_chunk = n_tok // PEER_TOK_CHUNK
    h_c = h.reshape(n_chunk, PEER_TOK_CHUNK, d)
    e_c = expert.reshape(n_chunk, PEER_TOK_CHUNK, n_sel)
    g_c = gates.reshape(n_chunk, PEER_TOK_CHUNK, n_sel)

    def one_chunk(args):
        hc, ec, gc = args
        act = jax.nn.gelu(jnp.einsum('td,ted->te', hc, u[ec]).astype(f32), approximate=False)
        return jnp.einsum('te,ted->td', (gc * act).astype(v.dtype), v[ec])

    out = lax.map(one_chunk, (h_c, e_c, g_c))
    return out.reshape(bsz, s, d).astype(h.dtype)

def second_inputs(seed: int = 0) -> dict:
    key = jax.random.key(seed)
    ks = jax.random.split(key, 24)
    f32 = jnp.float32
    D = D_MODEL

    def nrm(k, shape, scale):
        return jax.random.normal(k, shape, f32) * scale

    def gain(k, shape):
        return 1.0 + 0.02 * jax.random.normal(k, shape, f32)

    dt = jnp.exp(jax.random.uniform(ks[9], (N_EVEN, GDN_HEADS), f32, math.log(1e-3), math.log(1e-1)))
    return {
        'x': nrm(ks[0], (BATCH, SEQ, D), 1.0),
        'c': nrm(ks[1], (BATCH, D), 1.0),
        'positions': jnp.broadcast_to(jnp.arange(SEQ, dtype=jnp.int32), (BATCH, SEQ)),
        'mod_w': nrm(ks[2], (DEPTH, D, 6 * D), 0.5 * D ** -0.5),
        'mod_b': nrm(ks[3], (DEPTH, 6 * D), 0.02),
        'norm_mix': gain(ks[4], (DEPTH, D)),
        'norm_ffn': gain(ks[5], (DEPTH, D)),
        'hy_w_in': nrm(ks[6], (N_EVEN, D, HY_IN), D ** -0.5),
        'gdn_conv': nrm(ks[7], (N_EVEN, GDN_CONV, GDN_CONV_CH), GDN_CONV ** -0.5),
        'gdn_a_log': jnp.log(jax.random.uniform(ks[8], (N_EVEN, GDN_HEADS), f32, 1.0, 16.0)),
        'gdn_dt_bias': dt + jnp.log(-jnp.expm1(-dt)),
        'gdn_o_norm': gain(ks[10], (N_EVEN, GDN_DV)),
        'hy_w_out': nrm(ks[11], (N_EVEN, HY_OUT, D), HY_OUT ** -0.5),
        'mla_w_in': nrm(ks[12], (N_ODD, D, MLA_IN), D ** -0.5),
        'mla_q_norm': gain(ks[13], (N_ODD, MLA_Q_RANK)),
        'mla_kv_norm': gain(ks[14], (N_ODD, MLA_KV_RANK)),
        'mla_w_uq': nrm(ks[15], (N_ODD, MLA_Q_RANK, MLA_HEADS * (MLA_NOPE + MLA_ROPE)), MLA_Q_RANK ** -0.5),
        'mla_w_ukv': nrm(ks[16], (N_ODD, MLA_KV_RANK, MLA_HEADS * (MLA_NOPE + MLA_V)), MLA_KV_RANK ** -0.5),
        'mla_w_out': nrm(ks[17], (N_ODD, MLA_HEADS * MLA_V, D), (MLA_HEADS * MLA_V) ** -0.5),
        'peer_w_q': nrm(ks[18], (DEPTH, D, PEER_HEADS * PEER_DKEY), D ** -0.5),
        'peer_sub_keys': nrm(ks[19], (DEPTH, PEER_HEADS, 2, PEER_NKEYS, PEER_DKEY // 2), (PEER_DKEY // 2) ** -0.5),
        'peer_u': nrm(ks[20], (DEPTH, PEER_EXPERTS, D), D ** -0.5),
        'peer_v': nrm(ks[21], (DEPTH, PEER_EXPERTS, D), PEER_HEADS ** -0.5),
        'final_norm': gain(ks[22], (D,)),
    }

def second_block(x, c, positions, mod_w, mod_b, norm_mix, norm_ffn, hy_w_in, gdn_conv, gdn_a_log,
              gdn_dt_bias, gdn_o_norm, hy_w_out, mla_w_in, mla_q_norm, mla_kv_norm, mla_w_uq,
              mla_w_ukv, mla_w_out, peer_w_q, peer_sub_keys, peer_u, peer_v, final_norm):
    cond = jax.nn.silu(c)
    cos_b, sin_b = rope_tables(positions, MOBA_DH)
    cos_c, sin_c = rope_tables(positions, MLA_ROPE)
    for layer in range(DEPTH):
        mod = cond @ mod_w[layer] + mod_b[layer]
        sh1, sc1, g1, sh2, sc2, g2 = jnp.split(mod[:, None, :], 6, axis=-1)
        h = rmsnorm(x, norm_mix[layer]) * (1.0 + sc1) + sh1
        i = layer // 2
        if layer % 2 == 0:
            y = hybrid_mixer(h, cos_b, sin_b, hy_w_in[i], gdn_conv[i], gdn_a_log[i], gdn_dt_bias[i],
                             gdn_o_norm[i], hy_w_out[i])
        else:
            y = mla_mixer(h, cos_c, sin_c, mla_w_in[i], mla_q_norm[i], mla_kv_norm[i], mla_w_uq[i],
                          mla_w_ukv[i], mla_w_out[i])
        x = x + g1 * y
        h = rmsnorm(x, norm_ffn[layer]) * (1.0 + sc2) + sh2
        x = x + g2 * peer_ffn(h, peer_w_q[layer], peer_sub_keys[layer], peer_u[layer], peer_v[layer])
    return rmsnorm(x, final_norm)


def setup_inputs(seed=0):
    out = dict(first_inputs(seed))
    for name, value in second_inputs(seed + 1).items():
        if name != "x":
            out[name + "_2"] = value
    return out


def reference(
    x, positions, attn_norm_g, w_in, rwkv_mu, rwkv_w0, rwkv_w2, rwkv_a0, rwkv_a2, rwkv_g2,
    rwkv_k_k, rwkv_k_a, rwkv_r_k, rwkv_ln_g, rwkv_ln_b, pool_w, pool_scale, ret_gn_g, gate_b,
    w_branch, w_out, mlp_norm_g, mlp_up, mlp_down, final_norm_g, c_2, positions_2, mod_w_2,
    mod_b_2, norm_mix_2, norm_ffn_2, hy_w_in_2, gdn_conv_2, gdn_a_log_2, gdn_dt_bias_2,
    gdn_o_norm_2, hy_w_out_2, mla_w_in_2, mla_q_norm_2, mla_kv_norm_2, mla_w_uq_2, mla_w_ukv_2,
    mla_w_out_2, peer_w_q_2, peer_sub_keys_2, peer_u_2, peer_v_2, final_norm_2,
):
    x = first_block(
        x, positions, attn_norm_g, w_in, rwkv_mu, rwkv_w0, rwkv_w2, rwkv_a0, rwkv_a2, rwkv_g2,
        rwkv_k_k, rwkv_k_a, rwkv_r_k, rwkv_ln_g, rwkv_ln_b, pool_w, pool_scale, ret_gn_g,
        gate_b, w_branch, w_out, mlp_norm_g, mlp_up, mlp_down, final_norm_g,
    )
    return second_block(
        x, c_2, positions_2, mod_w_2, mod_b_2, norm_mix_2, norm_ffn_2, hy_w_in_2, gdn_conv_2,
        gdn_a_log_2, gdn_dt_bias_2, gdn_o_norm_2, hy_w_out_2, mla_w_in_2, mla_q_norm_2,
        mla_kv_norm_2, mla_w_uq_2, mla_w_ukv_2, mla_w_out_2, peer_w_q_2, peer_sub_keys_2,
        peer_u_2, peer_v_2, final_norm_2,
    )


_drawn_inputs = setup_inputs


def setup_inputs(seed=0):
    import zlib

    import numpy as np

    out = dict(_drawn_inputs(seed))
    spreads = {}
    factors = {'rwkv_w2': 2.946,
     'rwkv_a0': 2.865,
     'rwkv_k_k': 2.706,
     'norm_mix_2': 6.007,
     'norm_ffn_2': 4.68,
     'gdn_a_log_2': 3.624,
     'gdn_o_norm_2': 8.0,
     'mla_q_norm_2': 8.0,
     'mla_kv_norm_2': 8.0,
     'final_norm_2': 2.958}
    for name, (base, spread) in spreads.items():
        noise = np.random.default_rng([zlib.crc32(name.encode()), seed]).standard_normal(out[name].shape)
        drawn = base * np.exp(spread * noise) if base else spread * noise
        out[name] = jnp.asarray(drawn.astype(out[name].dtype))
    for name, factor in factors.items():
        out[name] = (out[name] * factor).astype(out[name].dtype)
    return out
```

```python
from collections import defaultdict
from contextlib import ExitStack

import numpy as np
import concourse.bass as bass
from concourse import mybir

F32 = mybir.dt.float32
F32R = mybir.dt.float32r
U32 = mybir.dt.uint32
I32 = mybir.dt.int32
ALU = mybir.AluOpType
ACT = mybir.ActivationFunctionType
AX = mybir.AxisListType

P = 128
S = 256
TT = S // P
D = 1024
KD = D // P
DEPTH = 2
BW = 512
KB = BW // P
CH = 64
DFF = 4096
A0, B0, C0, D0, G0 = 0, 1092, 2788, 3300, 4836
TOPK = 64
NEXP = 16384
NKEY = 128
PH, PK = 8, 16
RING = 8
BANKS = 3
MOD = 6 * KD
BIG = 1e30
FILL = -1e38
TAKEN = -3e38

CONST_COLS = [("ident", 128), ("bones", 128), ("ones", 128), ("rot_att", 128), ("rot_ret", 128), ("rot_moba", 128),
              ("rot_mla", 128), ("mask_neg", 256), ("mask_pos", 256), ("mask_low_neg", 128), ("tri01", 128),
              ("tri_fill", 128), ("tri_bias", 128), ("causal_bias1", 256), ("chunk_low_bias", 128), ("chunk_low", 128),
              ("iota", 128), ("freq", 4), ("pool_first", 64)]
CONST_AT, _at = {}, 0
for _name, _n in CONST_COLS:
    CONST_AT[_name] = (_at, _n)
    _at += _n
NCONST = _at


def rotation(period, rot):
    m = np.zeros((P, P), np.float32)
    half = rot // 2
    for base in range(0, P, period):
        for i in range(half):
            m[base + half + i, base + i] = -1.0
            m[base + i, base + half + i] = 1.0
    return m


def constants():
    c = np.zeros((P, NCONST), np.float32)

    def put(name, a):
        at, n = CONST_AT[name]
        c[:, at:at + n] = a

    i = np.arange(P)
    same = (i[:, None] // CH) == (i[None, :] // CH)
    upper = (i[:, None] < i[None, :]) & same
    upper_in = (i[:, None] <= i[None, :]) & same
    lower_in = (i[:, None] >= i[None, :])
    put("ident", np.eye(P))
    put("bones", same)
    put("ones", 1.0)
    put("rot_att", rotation(64, 16))
    put("rot_ret", rotation(32, 32))
    put("rot_moba", rotation(128, 128))
    put("rot_mla", rotation(64, 64))
    put("mask_neg", np.concatenate([-1.0 * upper, upper_in], 1))
    put("mask_pos", np.concatenate([upper, upper_in], 1))
    put("mask_low_neg", -1.0 * upper.T)
    put("tri01", lower_in)
    put("tri_fill", np.where(lower_in, 0.0, FILL))
    put("tri_bias", np.where(lower_in, 0.0, -BIG))
    put("causal_bias1", np.concatenate([np.zeros((P, P)), np.where(lower_in, 0.0, -BIG)], 1))
    put("chunk_low_bias", np.where(upper_in.T, 0.0, -BIG))
    put("chunk_low", upper.T)
    put("iota", np.tile(np.arange(P), (P, 1)))
    f_att = 500000.0 ** (-np.arange(0, 16, 2) / 16)
    f_ret = 1.0 / (10000.0 ** np.linspace(0.0, 1.0, 16))
    f_moba = 10000.0 ** (-np.arange(0, 128, 2) / 128)
    f_mla = 10000.0 ** (-np.arange(0, 64, 2) / 64)
    r64 = i % 64
    put("freq", np.stack([np.where(r64 < 16, f_att[r64 % 8], 0.0), f_ret[i % 16], f_moba[i % 64], f_mla[i % 32]], 1))
    t = np.arange(16) + 1.0
    put("pool_first", np.tile(np.concatenate([1.0 / np.minimum(t, w) for w in (2, 4, 8, 16)]), (P, 1)))
    return c


def retention_decay():
    gamma = 1.0 - 2.0 ** (-5.0 - np.arange(8, dtype=np.float64))
    diff = np.arange(S)[None, :] - np.arange(P)[:, None]
    full = np.where(diff[:, None, :] >= 0, gamma[None, :, None] ** np.maximum(diff, 0)[:, None, :], 0.0) * 32 ** -0.5
    return np.concatenate([full, full[:, :, :P]], 2).astype(np.float32).reshape(P, 8 * 384)


def rows_of(spec):
    at, out = 0, {}
    for name, n in spec:
        out[name] = (at, n)
        at += n
    assert at <= P
    return out


VEC1 = rows_of([("attn_norm_g", 8), ("mlp_norm_g", 8), ("rwkv_w0", 4), ("rwkv_a0", 4), ("rwkv_k_k", 4), ("rwkv_k_a", 4),
                ("rwkv_r_k", 4), ("rwkv_ln_g", 4), ("rwkv_ln_b", 4), ("pool_scale", 4), ("ret_gn_g", 4), ("gate_b", 32),
                ("mu_r", 4), ("mu_wd", 1), ("mu_k", 4), ("mu_v", 4), ("mu_ad", 1), ("mu_gd", 1)])
VEC2 = rows_of([("norm_mix0", 8), ("norm_ffn0", 8), ("mod_b0", 48), ("norm_mix1", 8), ("norm_ffn1", 8), ("mod_b1", 48)])
VEC3 = rows_of([("conv", 48), ("gdn_o_norm", 1), ("mla_q_norm", 4), ("mla_kv_norm", 2), ("final_norm_g", 8),
                ("final_norm_2", 8), ("c", 8)])
SHIFTED = [("wd", 512, 32), ("ad", 1568, 32), ("gd", 1600, 96), ("r", 0, 512), ("k", 544, 512), ("v", 1056, 512)]


class Counts:

    def __init__(self):
        self.seen, self.uses = defaultdict(int), defaultdict(int)

    def next(self, name, n=1):
        self.seen[name] += n
        return self.seen[name]

    def reused(self, name, buffers):
        self.uses[name] += 1
        return self.uses[name] > buffers

    def freed(self, name, buffers):
        return self.uses[name] - buffers


def positive(n):
    return not isinstance(n, int) or n > 0


def two_stacks(nc, io, out):
    ctx = ExitStack()
    with ctx:
        sems = {}

        def sem(name):
            if name not in sems:
                sems[name] = ctx.enter_context(nc.semaphore(name))
            return sems[name]

        address = {}

        def sb(name, shape, dt=F32):
            t = ctx.enter_context(nc.sbuf_tensor(name, shape, dt))[(slice(None),) * len(shape)]
            address[name] = nc.sbuf_base - 4 * int(np.prod(shape[1:]))
            return t

        def rounded(name, over, first, shape):
            t = nc.alloc_sbuf_tensor_at(name, shape, F32R, offset=address[over] + 4 * first)
            return t[(slice(None),) * len(shape)]

        arena = sb("arena", [P, 32768])
        ring = sb("ring", [P, RING, 1024])
        xT = sb("xT", [P, KD, S])
        hT = sb("hT", [P, KD, S])
        cst = sb("cst", [P, NCONST])
        vec = sb("vec", [P, 4, P])
        tab = sb("tab", [P, 2, 2, S])
        uT = sb("uT", [P, 2, 1024])
        selT = sb("selT", [P, 4, S])
        wT = sb("wT", [P, 2, S])
        mod = sb("mod", [P, DEPTH, MOD])
        cond = sb("cond", [P, 8])
        small = sb("small", [P, 128])
        gelu = tab[:, 0, :, :]
        w_high, w_low = rounded("w_high", "wT", 0, [P, 2, S]), rounded("w_low", "tab", 0, [P, 2, S])
        u_parts = rounded("u_parts", "uT", 0, [P, 2, 1024])
        v_high = rounded("v_high", "selT", 0, [P, 1024])
        v_low = rounded("v_low", "ring", 2 * 1024, [P, 4, 1024])
        h_high, h_low = rounded("h_high", "ring", 6 * 1024, [P, KD, S]), rounded("h_low", "hT", 0, [P, KD, S])

        PB = [ctx.enter_context(nc.psum_tensor(f"bank{i}", [P, 512], F32)) for i in range(8)]

        def C(name):
            at, n = CONST_AT[name]
            return cst[:, at:at + n]

        def area(at, *dims):
            n = int(np.prod(dims))
            v = arena[:, at:at + n]
            if len(dims) == 2:
                v = v.rearrange("p (a b) -> p a b", b=dims[1])
            if len(dims) == 3:
                v = v.rearrange("p (a b c) -> p a b c", b=dims[1], c=dims[2])
            if len(dims) == 4:
                v = v.rearrange("p (a b c d) -> p a b c d", b=dims[1], c=dims[2], d=dims[3])
            return v

        def vcol(tile, rows, name, j=0):
            return vec[:, tile, rows[name][0] + j:rows[name][0] + j + 1]

        units = []
        tiles = {}
        mod_unit = {}
        stage_units = {}

        def unit_of(src, rows, k, n, dup=1):
            return [(rows, k, n * d, n, src, n * dup) for d in range(dup)]

        def tile(label, unit_list, n):
            tiles[label] = (len(tiles), len(units), len(unit_list), n)
            units.extend(unit_list)

        def columns(w, c0, n, dup=1):
            return unit_of(w[:, c0:c0 + n].rearrange("(k p) n -> p k n", p=P), P, w.shape[0] // P, n, dup)

        for l in range(DEPTH):
            w = io["w_in"][l]
            for g in range(2):
                tile(("k", l, g), [columns(w, A0 + 512 + 64 * g, 64, 2)], P)
            for j in range(4):
                tile(("q", l, j), [columns(w, A0 + P * j, P)], P)
            for j in range(2):
                tile(("qi", l, j), [columns(w, A0 + 768 + P * j, P)], P)
            tile(("ki", l), [columns(w, A0 + 1024, 64, 2)], P)
            for g in range(2):
                tile(("v", l, g), [columns(w, A0 + 640 + 64 * g, 64, 2)], P)
            tile(("wi", l), [columns(w, A0 + 1088, 4)], 4)
            for j in range(2):
                tile(("rq", l, j), [columns(w, D0 + P * j, P)], P)
            for j in range(2):
                tile(("rk", l, j), [columns(w, D0 + 256 + P * j, P)], P)
            for j in range(4):
                tile(("rv", l, j), [columns(w, D0 + 512 + P * j, P)], P)
            for j in range(4):
                tile(("pc", l, j), [columns(w, C0 + P * j, P)], P)
            for name, c0, n in SHIFTED:
                for j in range(-(-n // P)):
                    tile(("s" + name, l, j), [columns(w, B0 + c0 + P * j, min(P, n))], min(P, n))
            for j in range(4):
                tile(("rg", l, j), [columns(w, D0 + 1024 + P * j, P)], P)
            for j in range(MOD):
                mod_unit[l, j] = len(units)
                units.append(columns(io["mod_w_2"][l], P * j, P))
            stage_units[10 * l + 1] = len(units)
            for j in range(4):
                tile(("pool", l, j), [unit_of(io["pool_w"][l, j].rearrange("(k p) n -> p k n", p=P), P, 1, P)], P)
            stage_units[10 * l + 4] = len(units)
            for name, src, r in (("w2", "rwkv_w2", 32), ("a2", "rwkv_a2", 32), ("g2", "rwkv_g2", 96)):
                for j in range(4):
                    tile((name, l, j), [unit_of(io[src][l, :, P * j:P * j + P].rearrange("(k p) n -> p k n", p=r),
                                                r, 1, P)], P)
            stage_units[10 * l + 5] = stage_units[10 * l + 6] = len(units)
            for m in range(KD):
                for b in range(4):
                    tile(("gate", l, m, b), [columns(w, G0 + D * b + P * m, P)], P)
                    tile(("branch", l, m, b), [columns(io["w_branch"][l, b], P * m, P)], P)
            for m in range(KD):
                tile(("wout", l, m), [columns(io["w_out"][l], P * m, P)], P)
            stage_units[10 * l + 7] = len(units)
            for j in range(DFF // P):
                tile(("up", l, j), [columns(io["mlp_up"][l], P * j, P)], P)
            for m in range(KD):
                tile(("down", l, m), [columns(io["mlp_down"][l, D * q:D * q + D, :], P * m, P)
                                      for q in range(DFF // D)], P)
            stage_units[10 * l + 8] = len(units)
        stage_units[20] = len(units)
        for l in range(DEPTH):
            if l == 0:
                w = io["hy_w_in_2"][0]
                for j in range(12):
                    tile(("conv", j), [columns(w, P * j, P)], P)
                tile(("ba",), [columns(w, 2048, 8)], 8)
                for j in range(4):
                    tile(("z", j), [columns(w, 1536 + P * j, P)], P)
                for j in range(4):
                    tile(("mq", j), [columns(w, 2056 + P * j, P)], P)
                for j in range(4):
                    tile(("mk", j), [columns(w, 2568 + P * j, P)], P)
                for j in range(4):
                    tile(("mv", j), [columns(w, 3080 + P * j, P)], P)
                stage_units[21] = stage_units[22] = stage_units[23] = len(units)
                for m in range(KD):
                    tile(("mix", l, m), [columns(io["hy_w_out_2"][0], P * m, P)], P)
            else:
                w = io["mla_w_in_2"][0]
                for j in range(6):
                    tile(("c", j), [columns(w, P * j, P)], P)
                tile(("kr",), [columns(w, 768, 64, 2)], P)
                uq, ukv = io["mla_w_uq_2"][0], io["mla_w_ukv_2"][0]
                for h in range(8):
                    tile(("qn", h), [columns(uq, 192 * h, P)], P)
                for j in range(4):
                    two = [(P, 4, 64 * d, 64, uq[:, 192 * (2 * j + d) + P:192 * (2 * j + d) + 192].rearrange(
                        "(k p) n -> p k n", p=P), P) for d in range(2)]
                    tile(("qr", j), [two], P)
                for h in range(8):
                    tile(("kn", h), [columns(ukv, 256 * h, P)], P)
                for h in range(8):
                    tile(("lv", h), [columns(ukv, 256 * h + P, P)], P)
                stage_units[31] = stage_units[32] = stage_units[33] = len(units)
                for m in range(KD):
                    tile(("mix", l, m), [columns(io["mla_w_out_2"][0], P * m, P)], P)
            stage_units[24 + 10 * l] = len(units)
            for j in range(16):
                tile(("pq", l, j), [columns(io["peer_w_q_2"][l], P * j, P)], P)
            for j in range(4):
                sk = io["peer_sub_keys_2"][l].rearrange("h s n d -> (h s) n d")
                tile(("sub", l, j), [unit_of(sk[4 * j:4 * j + 4].rearrange("a n d -> n a d"), P, 4, P)], P)
            stage_units[25 + 10 * l] = stage_units[26 + 10 * l] = len(units)
            stage_units[27 + 10 * l] = len(units)

        loads_in_slot = [0] * RING
        unit_full = []
        for n, u in enumerate(units):
            loads_in_slot[n % RING] += 16 * len(u)
            unit_full.append(loads_in_slot[n % RING])

        def slot_view(n, rows, k, width):
            return ring[0:rows, n % RING, 0:k * width].rearrange("p (k n) -> p k n", n=width)

        def bank_of(label):
            return PB[tiles[label][0] % BANKS]

        def last_unit(label):
            return tiles[label][1] + tiles[label][2]

        oB, oA, oC, oD = (area(1024 * i, 4, S) for i in range(4))
        branch_out = [oA, oB, oC, oD]
        raw = {}
        shifted = {}
        at = 4096
        for name, _, n in SHIFTED:
            raw[name] = area(at, -(-n // P), S + 1)
            at += -(-n // P) * (S + 1)
        raw_end = at
        for name, _, n in SHIFTED:
            shifted[name] = area(at, -(-n // P), S)
            at += -(-n // P) * S
        rw_at = at
        square = area(30720, KD, S)
        W0 = 18432
        q_t = area(W0, 4, S)
        k_t = area(W0 + 1024, 2, S)
        v_t = area(W0 + 1536, 2, TT, P)
        qi_t = area(W0 + 2048, 2, S)
        ki_t = area(W0 + 2560, 1, S)
        wi_t = area(W0 + 2816, TT, 4)
        rq_t = area(W0 + 2880, 2, S)
        rk_t = area(W0 + 3392, 2, S)
        rv_t = area(W0 + 3904, 4, TT, P)
        rg_t = area(W0 + 4928, 4, S)
        pc_t = area(W0 + 5952, 4, S + 16)
        pool_a = area(W0 + 7040, 1, S + 16)
        pool_b = area(W0 + 7312, 1, S + 16)
        pooled = area(W0 + 7584, 4, S)
        decay_t = area(W0 + 8608, 8, 384)
        idx = area(W0 + 11680, 1, S)
        work = area(W0 + 11936, 1, S)
        selbias = area(W0 + 12192, TT, S)
        probs = area(W0 + 12704, 2, S)
        probsT = area(W0 + 13216, 2, S)
        rope_tmp = area(W0 + 13728, 2, S)
        ret_s = area(W0 + 11680, 2, 384)
        gn_sq = area(W0 + 0, 4, S)
        gn_rs = area(W0 + 1024, 4, S)

        mx, nmx, den, rden = (small[:, 2 * i:2 * i + 2] for i in range(4))
        m8 = small[:, 8:16]
        cnt, need = small[:, 16:17], small[:, 17:18]

        rk_prep = {}
        at = rw_at
        for name in ("ld", "a", "g", "kk", "L"):
            rk_prep[name] = area(at, 4, S)
            at += 1024
        LD, RA, RG, KK, RL = (rk_prep[x] for x in ("ld", "a", "g", "kk", "L"))
        assert at <= W0, at
        EP, EN, EX = area(4096, 4, S), area(5120, 4, S), area(6144, 4, S)
        assert 7168 <= raw_end
        at = W0
        KR = area(at, 8, 2, P)
        at += 2048
        BMb = area(at, 8, P)
        KMb = area(at + 1024, 8, P)
        VD = area(at + 2048, 8, P)
        TOK = area(at + 3072, 8, 3, P)
        at += 6144
        ARb = area(at, 8, P)
        KK2 = area(at + 1024, 8, 2, P)
        at += 3072
        MS = area(at, 8, P)
        MT = area(at + 1024, 8, P)
        INV = area(at + 2048, 8, P)
        at += 3072
        assert at <= 32768, at
        ST = uT[:, 0, 0:512].rearrange("p (a b) -> p a b", b=P)
        RHS = uT[:, 0, 512:1024].rearrange("p (a b) -> p a b", b=P)
        US = uT[:, 1, 0:512].rearrange("p (a b) -> p a b", b=P)
        STMP = uT[:, 1, 512:1024].rearrange("p (a b) -> p a b", b=P)
        cond_at = uT[:, 0, 0:KD * (2 * MOD - 1)].rearrange("p (k n) -> p k n", n=2 * MOD - 1)
        mod_rows = uT[0:MOD, 1, 0:P]
        YT = EX


        rows_in = area(8192, 4, P)
        x_in = area(0, TT, D)
        ipos = arena[:, 8704:9216].bitcast(I32).rearrange("p (a b) -> p a b", b=S)
        merged = area(8192, KD, S)
        gate_s = area(10240, 4, S)
        proj_s = area(11264, 4, S)
        prod_s = area(12288, 1, S)
        res_s = area(12544, 4, S)
        up_t = area(13568, 32, S)
        rstd = selT[:, 0, :]
        mix_t = area(0, KD, S)
        conv_in = area(2048, 12, S + 3)
        gqkv = area(5156, 12, S)
        gq, gk, gv = gqkv[:, 0:4, :], gqkv[:, 4:8, :], gqkv[:, 8:12, :]
        z_t = area(8228, 4, S)
        mq_t, mk_t = area(9252, 4, S), area(10276, 4, S)
        mv_t = area(11300, 4, TT, P)
        gsq = area(12324, 8, S)
        gcols = area(14372, 8, P)
        dmat = area(15396, 8, P)
        erow = area(16420, 4, S)
        qk_t = area(14372, 8, P)
        qk2_t = area(W0, 8, P)
        vb_t, kb_t, kd_t = area(W0 + 1024, 8, P), area(W0 + 2048, 8, P), area(W0 + 3072, 8, P)
        uw_t = area(W0 + 4096, 8, 2 * P)
        w_t = uw_t[:, :, P:2 * P]
        GS = area(W0 + 6144, 4, P)
        vn_t = area(W0 + 6656, 4, P)
        ba_t = area(W0 + 7168, TT, 8)
        gl_t = area(W0 + 7184, TT, 8)
        glog = area(W0 + 7200, TT, 4)
        beta_t = area(W0 + 7208, TT, 4)
        sp_t = area(W0 + 7216, 3, TT, 4)
        eg_t = area(W0 + 7240, 3, TT, 4)
        ab_t = area(W0 + 7264, 1, 8)
        lat = area(2048, 6, S)
        lat_sq = area(3584, 6, S)
        kr_t = area(5120, 1, S)
        qn_t, qr_t, kn_t = area(5376, 8, S), area(7424, 4, S), area(8448, 8, S)
        lv_t = area(10496, 8, TT, P)
        kr2_t = area(12544, 2, S)
        res2_s = area(W0 + 7808, 4, S)
        pq_t = area(0, 16, S)
        sub_t = area(4096, 16, P)
        key_t = area(6144, TT, 16, P)
        key_s = area(10240, 2, P)
        tv = area(10496, 16, 16)
        ti = arena[:, 10752:11008].bitcast(U32).rearrange("p (a b) -> p a b", b=16)
        tif = area(11008, 16, 16)
        cand = area(11264, 8, S)
        cand_s = area(13312, 2, S)
        cv = area(13824, TT, 8, 16)
        ci = arena[:, 14080:14208].bitcast(U32).rearrange("p (a b) -> p a b", b=16)
        ci_row = arena[:, 14208:14336].bitcast(U32).rearrange("p (a b) -> p a b", b=16)
        second = area(14336, 8, 16)
        first_k = area(14464, 8, 16)
        hot = area(14592, 8, S)
        pick_t = area(16640, 3, TT, P)
        esum = area(17408, 2, TT, 8)
        gates = arena[:, :].rearrange("p (t e) -> p t e", e=NKEY)
        one_d = uT[:, 0, :].rearrange("p (b t e) -> p b t e", b=2, t=4)
        one_p = uT[:, 1, :].rearrange("p (b t e) -> p b t e", b=2, t=4)
        moe_t = area(0, TT, D)
        out_t = area(0, TT, D)

        def first_tiles(l):
            out = [("k", l, g) for g in range(2)] + [("q", l, j) for j in range(4)] + [("qi", l, j) for j in range(2)]
            out += [("ki", l)] + [("v", l, g) for g in range(2)] + [("wi", l)]
            return out + [(name, l, j) for name in ("rq", "rk") for j in range(2)]

        def later_tiles(l):
            out = [(name, l, j) for name in ("rv", "pc") for j in range(4)]
            out += [("s" + name, l, j) for name, _, n in SHIFTED for j in range(-(-n // P))]
            return out + [("rg", l, j) for j in range(4)]

        ROPE_FILL, INDEXER_FILL = 6, (4, 9)
        INDEXER_END = ROPE_FILL + sum(INDEXER_FILL)

        def attention_fill(l):
            rest = later_tiles(l)[INDEXER_END:]
            return [[label] for label in rest] + [[("mod", l, 4 * j + i) for i in range(4)] for j in range(8)]

        def place_of(label):
            kind, j = label[0], label[2] if len(label) > 2 else 0
            if kind == "wi":
                return wi_t
            if kind == "pc":
                return pc_t[:, j, 16:16 + S]
            if kind[0] == "s":
                return raw[kind[1:]][0:tiles[label][3], j, 1:1 + S]
            if kind in ("v", "rv"):
                return {"v": v_t, "rv": rv_t}[kind][:, j, :, :]
            return {"k": k_t, "q": q_t, "qi": qi_t, "ki": ki_t, "rq": rq_t, "rk": rk_t, "rg": rg_t}[kind][:, j, :]

        def att_rope(l):
            out = [(k_t[:, g, :], ("k", l, g), "rot_att") for g in range(2)]
            out += [(q_t[:, j, :], ("q", l, j), "rot_att") for j in range(4)]
            out += [(qi_t[:, j, :], ("qi", l, j), "rot_att") for j in range(2)]
            return out + [(ki_t[:, 0, :], ("ki", l), "rot_att")]

        def ret_rope(l):
            return ([(rq_t[:, j, :], ("rq", l, j), "rot_ret") for j in range(2)]
                    + [(rk_t[:, j, :], ("rk", l, j), "rot_ret") for j in range(2)])

        def moba_rope():
            return ([(mq_t[:, j, :], ("mq", j), "rot_moba") for j in range(4)]
                    + [(mk_t[:, j, :], ("mk", j), "rot_moba") for j in range(4)])

        def mla_rope():
            return [(qr_t[:, j, :], ("qr", j), "rot_mla") for j in range(4)] + [(kr_t[:, 0, :], ("kr",), "rot_mla")]

        def dsa_jobs():
            out = []
            for i in range(TT):
                for h in range(8):
                    r, g, q, ns = slice(64 * (h % 2), 64 * (h % 2) + 64), h // 4, slice(i * P, i * P + P), P * (i + 1)
                    out.append(dict(scores=[(q_t[r, h // 2, q], k_t[r, g, 0:ns])], ns=ns, scale=64 ** -0.5,
                                    bias=selbias[:, i, 0:ns], values=[v_t[:, g, t, :] for t in range(i + 1)],
                                    rows=r, dest=oA[r, h // 2, q]))
            return out

        def causal_bias(i):
            return C("tri_bias") if i == 0 else C("causal_bias1")

        def moba_jobs():
            out = []
            for h in range(4):
                for i in range(TT):
                    q, ns = slice(i * P, i * P + P), P * (i + 1)
                    out.append(dict(scores=[(mq_t[:, h, q], mk_t[:, h, 0:ns])], ns=ns, scale=128 ** -0.5,
                                    bias=causal_bias(i), values=[mv_t[:, h, t, :] for t in range(i + 1)],
                                    rows=slice(0, P), dest=mix_t[:, 4 + h, q]))
            return out

        def mla_jobs():
            out = []
            for h in range(8):
                for i in range(TT):
                    q, ns = slice(i * P, i * P + P), P * (i + 1)
                    out.append(dict(scores=[(qn_t[:, h, q], kn_t[:, h, 0:ns]), (qr_t[:, h // 2, q], kr2_t[:, h % 2, 0:ns])],
                                    ns=ns, scale=192 ** -0.5, bias=causal_bias(i),
                                    values=[lv_t[:, h, t, :] for t in range(i + 1)],
                                    rows=slice(0, P), dest=mix_t[:, h, q]))
            return out

        SETUP = 4 + DEPTH * (12 + len(SHIFTED) + 3) + 7
        angle_t = area(9216, 2, S)

        block = ctx.enter_context(nc.Block())

        @block.tensor
        def _(eng):
            pe = Counts()
            used = [0]

            def use(label):
                n = used[0]
                used[0] += 1
                eng.wait_ge(sem(f"w_full{n % RING}"), unit_full[n])
                return n

            def stream(label, moving, tokens=False, width=S):
                t, first, count, n = tiles[label]
                assert first == used[0], (label, first, used[0])
                if t + 1 > BANKS:
                    eng.wait_ge(sem("evac"), t + 1 - BANKS)
                ps = PB[t % BANKS]
                for u in range(count):
                    m = use(label)
                    rows, k, _, _, _, w = units[m][0]
                    wv = slot_view(m, rows, k, w)
                    if tokens:
                        for tt in range(TT):
                            for i in range(k):
                                ins = eng.matmul(ps[:, tt * P:tt * P + n], moving(i)[:, tt * P:tt * P + P], wv[:, i, :],
                                                 start=(i == 0), stop=(i == k - 1))
                    else:
                        for i in range(k):
                            ins = eng.matmul(ps[0:n, 0:width], wv[:, i, :], moving(u * 8 + i),
                                             start=(u == 0 and i == 0), stop=(u == count - 1 and i == k - 1))
                    ins.then_inc(sem("unit_done"), 1)

            def hidden(i):
                return hT[:, i, :]

            def norm_sum(sq, n):
                eng.wait_ge(sem("sq_ready"), pe.next("sq_ready"))
                if pe.reused("ss_read", 1):
                    eng.wait_ge(sem("ss_read"), pe.freed("ss_read", 1))
                for k in range(n):
                    ins = eng.matmul(PB[4][:, 0:S], C("ones"), sq[:, k, :], start=(k == 0), stop=(k == n - 1))
                ins.then_inc(sem("ss_ready"), 1)

            def rope(what, fill=()):
                for i, (ap, label, rot) in enumerate(what):
                    eng.wait_ge(sem("evac"), tiles[label][0] + 1)
                    j = pe.uses["rope_done"] % 2
                    if pe.reused("rope_done", 2):
                        eng.wait_ge(sem("rope_done"), pe.freed("rope_done", 2))
                    eng.matmul(PB[4 + j][:, 0:S], C(rot), ap, start=True, stop=True).then_inc(sem("rot_mm"), 1)
                    if i % 2 == 1 and i // 2 < len(fill):
                        project(fill[i // 2])

            def rope_finished():
                eng.wait_ge(sem("rope_done"), pe.uses["rope_done"])

            def modulate(l, j):
                n = used[0]
                assert n == mod_unit[l, j]
                used[0] += 1
                if j == 0:
                    eng.wait_ge(sem("cond_placed"), l + 1)
                eng.wait_ge(sem(f"w_full{n % RING}"), unit_full[n])
                wv = slot_view(n, P, KD, P)
                for i in range(KD):
                    ins = eng.matmul(PB[3][0:MOD, 0:P], cond_at[:, i, MOD - 1 - j:2 * MOD - 1 - j], wv[:, i, :],
                                     start=(j == 0 and i == 0), stop=(j == MOD - 1 and i == KD - 1))
                ins.then_inc(sem("unit_done"), 1)

            def project(label):
                if label[0] == "mod":
                    modulate(*label[1:])
                else:
                    stream(label, hidden, tokens=label[0] in ("v", "wi", "rv"))

            def attention(jobs, fill=()):
                def scores(j):
                    if pe.reused("sm_read", 2):
                        eng.wait_ge(sem("sm_read"), pe.freed("sm_read", 2))
                    job = jobs[j]
                    for i, (a, b) in enumerate(job["scores"]):
                        ins = eng.matmul(PB[6 + j % 2][:, 0:job["ns"]], a, b, start=(i == 0),
                                         stop=(i == len(job["scores"]) - 1))
                    ins.then_inc(sem("score_mm"), 1)

                def values(j):
                    job, ps = jobs[j], PB[4 + j % 2]
                    eng.wait_ge(sem("p_ready"), pe.next("p_ready"))
                    if pe.reused("pv_out", 2):
                        eng.wait_ge(sem("pv_out"), pe.freed("pv_out", 2))
                    for t in range(job["ns"] // P):
                        ins = eng.transpose(ps[:, t * P:t * P + P], probs[:, j % 2, t * P:t * P + P], C("ident"))
                    ins.then_inc(sem("pT_mm"), 1)
                    eng.wait_ge(sem("pT_ready"), pe.next("pT_ready"))
                    for t in range(job["ns"] // P):
                        ins = eng.matmul(ps[:, 256:384], job["values"][t], probsT[:, j % 2, t * P:t * P + P],
                                         start=(t == 0), stop=(t == job["ns"] // P - 1))
                    ins.then_inc(sem("pv_mm"), 1)

                scores(0)
                for j in range(len(jobs)):
                    if j + 1 < len(jobs):
                        scores(j + 1)
                    for label in fill[j] if fill else ():
                        project(label)
                    values(j)
                eng.wait_ge(sem("pv_out"), pe.uses["pv_out"])

            def group_norm(y):
                for t in range(4):
                    ins = eng.matmul(PB[4 + t // 2][:, (t % 2) * S:(t % 2) * S + S], C("bones"), y[:, t, :],
                                     start=True, stop=True)
                ins.then_inc(sem("gn_sum"), 1)
                eng.wait_ge(sem("gn_sq"), pe.next("gn_sq"))
                for t in range(4):
                    ins = eng.matmul(PB[6 + t // 2][:, (t % 2) * S:(t % 2) * S + S], C("bones"), gn_sq[:, t, :],
                                     start=True, stop=True)
                ins.then_inc(sem("gn_var"), 1)

            def inverse(blocks):
                groups = [list(range(g, g + 4)) for g in range(0, blocks, 4)]
                for n in range(5):
                    for g, blks in enumerate(groups):
                        if n < 4:
                            for i, b in enumerate(blks):
                                eng.matmul(PB[4 * g][:, i * P:i * P + P], MT[:, b, :], MS[:, b, :], start=True, stop=True)
                        for i, b in enumerate(blks):
                            ins = eng.matmul(PB[4 * g + 1][:, i * P:i * P + P], MS[:, b, :], MT[:, b, :],
                                             start=True, stop=True)
                        ins.then_inc(sem("sq_mm"), 1)
                    for g, blks in enumerate(groups):
                        if n < 4:
                            eng.wait_ge(sem("sq_ev"), pe.next("sq_ev"))
                        eng.wait_ge(sem("sqT_ev"), pe.next("sqT_ev"))
                        if pe.reused("inv_add", 2):
                            eng.wait_ge(sem("inv_add"), pe.freed("inv_add", 2))
                        for i, b in enumerate(blks):
                            ins = eng.matmul(PB[4 * g + 2][:, i * P:i * P + P], MT[:, b, :], INV[:, b, :],
                                             start=True, stop=True)
                        ins.then_inc(sem("inv_mm"), 1)
                eng.wait_ge(sem("inv_add"), pe.uses["inv_add"])

            def start_up():
                eng.wait_ge(sem("setup_in"), pe.next("setup_in", 16 * SETUP))
                for i in range(4):
                    eng.transpose(PB[0][:, i * P:i * P + P], rows_in[:, i, :], C("ident"))
                for tt in range(TT):
                    for k in range(KD):
                        ins = eng.transpose(PB[1 + k // 2][:, (k % 2) * S + tt * P:(k % 2) * S + tt * P + P],
                                            x_in[:, tt, k * P:k * P + P], C("ident"))
                ins.then_inc(sem("setup_mm"), 1)
                eng.wait_ge(sem("x_ready"), pe.next("x_ready"))

            def indexer(l):
                fill = later_tiles(l)[ROPE_FILL:INDEXER_END]
                for i in range(TT):
                    ns = P * (i + 1)
                    if pe.reused("idx_done", 1):
                        eng.wait_ge(sem("idx_done"), pe.freed("idx_done", 1))
                    for h in range(4):
                        r = slice(64 * (h % 2), 64 * (h % 2) + 64)
                        ins = eng.matmul(PB[6 + h % 2][:, (h // 2) * S:(h // 2) * S + ns],
                                         qi_t[r, h // 2, i * P:i * P + P], ki_t[r, 0, 0:ns], start=True, stop=True)
                    ins.then_inc(sem("idx_mm"), 1)
                    for label in fill[sum(INDEXER_FILL[:i]):sum(INDEXER_FILL[:i + 1])]:
                        project(label)
                eng.wait_ge(sem("idx_done"), pe.uses["idx_done"])

            def retention(l):
                for h in range(8):
                    r, t = slice(32 * (h % 4), 32 * (h % 4) + 32), h // 4
                    ps = PB[6 + h % 2]
                    if pe.reused("ret_s", 2):
                        eng.wait_ge(sem("ret_s"), pe.freed("ret_s", 2))
                    eng.matmul(ps[:, 0:S], rk_t[r, t, 0:P], rq_t[r, t, :], start=True, stop=True)
                    eng.matmul(ps[:, S:384], rk_t[r, t, P:S], rq_t[r, t, P:S],
                               start=True, stop=True).then_inc(sem("ret_mm"), 1)
                    for j in range(2):
                        modulate(l, 32 + 2 * h + j)
                    if h > 0:
                        retention_out(h - 1)
                retention_out(7)
                eng.wait_ge(sem("mod_rows"), l + 1)
                eng.transpose(PB[3][:, P:P + MOD], mod_rows, C("ident")[0:MOD, 0:MOD]).then_inc(sem("modT_mm"), 1)
                eng.wait_ge(sem("ret_out_ev"), pe.uses["ret_out_ev"])
                group_norm(oD)

            def retention_out(h):
                ps = PB[4 + h % 2]
                eng.wait_ge(sem("ret_s"), pe.next("ret_s"))
                if pe.reused("ret_out_ev", 2):
                    eng.wait_ge(sem("ret_out_ev"), pe.freed("ret_out_ev", 2))
                eng.matmul(ps[:, 0:P], rv_t[:, h // 2, 0, :], ret_s[:, h % 2, 0:P], start=True, stop=True)
                eng.matmul(ps[:, P:S], rv_t[:, h // 2, 0, :], ret_s[:, h % 2, P:S], start=True, stop=False)
                eng.matmul(ps[:, P:S], rv_t[:, h // 2, 1, :], ret_s[:, h % 2, S:384],
                           start=False, stop=True).then_inc(sem("ret_out_mm"), 1)

            def rwkv(l):
                eng.wait_ge(sem("lora_in"), pe.next("lora_in"))
                for name, src, r in (("w2", "wd", 32), ("a2", "ad", 32), ("g2", "gd", 96)):
                    for j in range(4):
                        stream((name, l, j), lambda i: shifted[src][0:r, 0, :])
                eng.wait_ge(sem("kk_sq"), pe.next("kk_sq"))
                for t in range(4):
                    ins = eng.matmul(PB[4 + t // 2][:, (t % 2) * S:(t % 2) * S + S], C("bones"), RL[:, t, :],
                                     start=True, stop=True)
                ins.then_inc(sem("kk_sum"), 1)
                eng.wait_ge(sem("bonus_in"), pe.next("bonus_in"))
                for t in range(4):
                    ins = eng.matmul(PB[6 + t // 2][:, (t % 2) * S:(t % 2) * S + S], C("bones"), LD[:, t, :],
                                     start=True, stop=True)
                ins.then_inc(sem("bonus_sum"), 1)
                eng.wait_ge(sem("evac"), tiles[("g2", l, 3)][0] + 1)
                for half in range(2):
                    eng.wait_ge(sem("blocks_ready"), pe.next("blocks_ready"))
                    if pe.uses["y_ev"] > 0:
                        eng.wait_ge(sem("y_ev"), pe.uses["y_ev"])
                    for b in range(8):
                        p0 = 4 * (b % 2)
                        if pe.reused("block_ev", 2):
                            eng.wait_ge(sem("block_ev"), pe.freed("block_ev", 2))
                        if pe.reused("tok_ev", 2):
                            eng.wait_ge(sem("tok_ev"), pe.freed("tok_ev", 2))
                        kr = KR[:, b, :, :].rearrange("p a b -> p (a b)")
                        eng.matmul(PB[p0][:, 0:S], BMb[:, b, :], kr, start=True, stop=True)
                        eng.matmul(PB[p0 + 1][:, 0:S], KMb[:, b, :], kr, start=True, stop=True)
                        eng.matmul(PB[p0 + 2][:, 0:P], KR[:, b, 0, :], BMb[:, b, :], start=True, stop=True)
                        for i, src in enumerate((BMb, KMb, VD)):
                            ins = eng.transpose(PB[p0 + 3][:, i * P:i * P + P], src[:, b, :], C("ident"))
                        ins.then_inc(sem("block_mm"), 1)
                    eng.wait_ge(sem("block_ev"), pe.uses["block_ev"])
                    eng.wait_ge(sem("tok_ev"), pe.uses["tok_ev"])
                    inverse(8)
                    for c in range(2):
                        last_chunk = half == 1 and c == 1
                        eng.wait_ge(sem("state_up"), pe.next("state_up"))
                        for p in range(4):
                            b, q = 2 * p + c, slice(p * P, p * P + P)
                            eng.matmul(PB[0][:, q], KR[:, b, 0, :], ST[:, p, :], start=True, stop=False)
                            ins = eng.matmul(PB[0][:, q], KK2[:, b, 0, :], TOK[:, b, 2, :], start=False, stop=True)
                        ins.then_inc(sem("rhs_mm"), 1)
                        eng.wait_ge(sem("rhs_ev"), pe.next("rhs_ev"))
                        for p in range(4):
                            ins = eng.matmul(PB[1][:, p * P:p * P + P], INV[:, 2 * p + c, :], RHS[:, p, :],
                                             start=True, stop=True)
                        ins.then_inc(sem("u_mm"), 1)
                        eng.wait_ge(sem("u_ev"), pe.next("u_ev"))
                        if pe.reused("y_ev", 1):
                            eng.wait_ge(sem("y_ev"), pe.freed("y_ev", 1))
                        for p in range(4):
                            b, q = 2 * p + c, slice(p * P, p * P + P)
                            eng.matmul(PB[2][:, q], ST[:, p, :], KR[:, b, 1, :], start=True, stop=False)
                            eng.matmul(PB[2][:, q], US[:, p, :], ARb[:, b, :], start=False, stop=False)
                            ins = eng.matmul(PB[2][:, q], TOK[:, b, 2, :], KK2[:, b, 1, :], start=False, stop=True)
                        if not last_chunk:
                            for p in range(4):
                                b, q = 2 * p + c, slice(p * P, p * P + P)
                                eng.matmul(PB[3][:, q], TOK[:, b, 0, :], US[:, p, :], start=True, stop=False)
                                ins = eng.matmul(PB[3][:, q], TOK[:, b, 1, :], TOK[:, b, 2, :], start=False, stop=True)
                        ins.then_inc(sem("state_mm"), 1)
                if pe.uses["y_ev"] > 0:
                    eng.wait_ge(sem("y_ev"), pe.uses["y_ev"])
                group_norm(YT)

            def experts(l):
                for j in range(16):
                    stream(("pq", l, j), hidden)
                for j in range(4):
                    t, first, count, n = tiles[("sub", l, j)]
                    if t + 1 > BANKS:
                        eng.wait_ge(sem("evac"), t + 1 - BANKS)
                    m = use(("sub", l, j))
                    for a in range(4):
                        ins = eng.transpose(PB[t % BANKS][:, a * P:a * P + P], slot_view(m, P, 4, P)[:, a, :], C("ident"))
                    ins.then_inc(sem("unit_done"), 1)
                eng.wait_ge(sem("evac"), tiles[("sub", l, 3)][0] + 1)
                for tt in range(TT):
                    for b in range(4):
                        if pe.reused("key_ev", 4):
                            eng.wait_ge(sem("key_ev"), pe.freed("key_ev", 4))
                        for a in range(4):
                            ins = eng.matmul(PB[4 + b][:, a * P:a * P + P], pq_t[:, 4 * b + a, tt * P:tt * P + P],
                                             sub_t[:, 4 * b + a, :], start=True, stop=True)
                        ins.then_inc(sem("key_mm"), 1)
                eng.wait_ge(sem("key_ev"), pe.uses["key_ev"])
                eng.wait_ge(sem("picked"), pe.next("picked"))
                for tt in range(TT):
                    for i in range(3):
                        ins = eng.transpose(PB[4 + i][:, tt * P:tt * P + P], pick_t[:, i, tt, :], C("ident"))
                ins.then_inc(sem("pickT_mm"), 1)
                eng.wait_ge(sem("pickT_ev"), pe.next("pickT_ev"))

            def gate_matrices(l):
                base = 64 * l

                def group(n, b):
                    if positive(n + (1 + base)):
                        eng.wait_ge(sem("one_rows"), n + (1 + base))
                    for j in range(4):
                        ins = eng.matmul(PB[b][:, j * P:j * P + P], one_p[:, b, j, :], one_d[:, b, j, :],
                                         start=True, stop=True)
                    ins.then_inc(sem("gate_mm"), 1)

                for b in range(2):
                    group(b, b)
                with eng.Fori(1, 32) as i:
                    for b in range(2):
                        if positive(i * 2 + (b - 1 + base)):
                            eng.wait_ge(sem("gate_ev"), i * 2 + (b - 1 + base))
                        group(i * 2 + b, b)
                eng.wait_ge(sem("gate_ev"), base + 64)

            def expert_tiles(l):
                base = NKEY * l

                def turn(e, j):
                    first_load = 16 + 1024 * l
                    n = 16 * (e // 2) + first_load if isinstance(e, int) else e * 8 + (first_load - 8 * (j % 2))
                    eng.wait_ge(sem(f"u_full{j % 2}"), n)
                    for q in range(2):
                        if positive(e * 2 + (2 * base + q - 1)):
                            eng.wait_ge(sem("uL_ready"), e * 2 + (2 * base + q - 1))
                        for k in range(4):
                            ins = eng.transpose(PB[4 + q][:, k * P:k * P + P],
                                                ring[:, j % 2, (4 * q + k) * P:(4 * q + k) * P + P], C("ident"))
                        ins.then_inc(sem("u_turned"), 1)

                def score(e, j):
                    b = j % 2
                    eng.wait_ge(sem("uL_ready"), e * 2 + (2 + 2 * base))
                    if positive(e + (base - 1)):
                        eng.wait_ge(sem("gelu_done"), e + (base - 1))
                    products = [(part, moving, k) for part, moving in ((1, h_high), (0, h_low), (0, h_high)) for k in range(KD)]
                    for i, (part, moving, k) in enumerate(products):
                        ins = eng.matmul(PB[6 + b][:, 0:S], u_parts[:, part, k * P:k * P + P], moving[:, k, :],
                                         start=(i == 0), stop=(i == len(products) - 1))
                    ins.then_inc(sem("exp_mm"), 1)

                def combine(e, j):
                    b = j % 2
                    eng.wait_ge(sem("wL_ready"), e + (1 + base))
                    eng.wait_ge(sem("vL_ready"), e + (1 + base))
                    first, last = (isinstance(e, int) and e == n for n in (0, NKEY - 1))
                    for tt in range(TT):
                        t = slice(tt * P, tt * P + P)
                        for q in range(2):
                            d = slice(q * 512, q * 512 + 512)
                            ps = PB[2 * tt + q][:, :]
                            eng.matmul(ps, w_low[:, b, t], v_high[:, d], start=first, stop=False)
                            eng.matmul(ps, w_high[:, b, t], v_low[:, j, d], start=False, stop=False)
                            ins = eng.matmul(ps, w_high[:, b, t], v_high[:, d], start=False, stop=last)
                    ins.then_inc(sem("v_free"), 1)

                eng.wait_ge(sem("h_split"), l + 1)
                turn(0, 0)
                for e in range(4):
                    turn(e + 1, (e + 1) % 4)
                    score(e, e)
                    if e > 0:
                        combine(e - 1, e - 1)
                with eng.Fori(1, 31) as i:
                    for j in range(4):
                        turn(i * 4 + (j + 1), (j + 1) % 4)
                        score(i * 4 + j, j)
                        combine(i * 4 + (j - 1), (j - 1) % 4)
                for j in range(4):
                    e = 124 + j
                    if e + 1 < NKEY:
                        turn(e + 1, (e + 1) % 4)
                    score(e, j)
                    combine(e - 1, (e - 1) % 4)
                combine(NKEY - 1, 3)
                eng.wait_ge(sem("experts0_ev"), pe.next("experts0_ev"))
                eng.wait_ge(sem("experts1_ev"), pe.next("experts1_ev"))
                for k in range(KD):
                    for tt in range(TT):
                        ins = eng.transpose(PB[4 + k // 2][:, (k % 2) * S + tt * P:(k % 2) * S + tt * P + P],
                                            moe_t[:, tt, k * P:k * P + P], C("ident"))
                ins.then_inc(sem("moe_mm"), 1)

            def gdn(l):
                eng.wait_ge(sem("gdn_sq"), pe.next("gdn_sq"))
                for j in range(8):
                    ins = eng.matmul(PB[4 + j // 2][:, (j % 2) * S:(j % 2) * S + S], C("ones"), gsq[:, j, :],
                                     start=True, stop=True)
                ins.then_inc(sem("l2_mm"), 1)
                eng.wait_ge(sem("gdn_gate"), pe.next("gdn_gate"))
                for tt in range(TT):
                    eng.matmul(PB[4][:, 8 * tt:8 * tt + 4], C("mask_pos")[:, P:S], glog[:, tt, :], start=True, stop=True)
                    ins = eng.matmul(PB[4][:, 8 * tt + 4:8 * tt + 8], C("bones"), glog[:, tt, :], start=True, stop=True)
                ins.then_inc(sem("gcum_mm"), 1)
                eng.wait_ge(sem("decay_rows"), pe.next("decay_rows"))
                for b in range(8):
                    ins = eng.transpose(PB[6 + b // 4][:, (b % 4) * P:(b % 4) * P + P], gcols[:, b, :], C("ident"))
                ins.then_inc(sem("grow_mm"), 1)
                eng.wait_ge(sem("gdn_qk"), pe.next("gdn_qk"))
                for b in range(8):
                    h, tt = b // 2, b % 2
                    ps = PB[4 + b % 2]
                    if pe.reused("gdn_tok", 2):
                        eng.wait_ge(sem("gdn_tok"), pe.freed("gdn_tok", 2))
                    q = slice(tt * P, tt * P + P)
                    eng.matmul(ps[:, 0:P], gk[:, h, q], gk[:, h, q], start=True, stop=True)
                    eng.matmul(ps[:, P:S], gq[:, h, q], gk[:, h, q], start=True, stop=True)
                    eng.transpose(ps[:, S:384], gk[:, h, q], C("ident"))
                    eng.transpose(ps[:, 384:512], gv[:, h, q], C("ident")).then_inc(sem("gdn_mm"), 1)
                for b in range(8):
                    ps = PB[b % 4]
                    eng.wait_ge(sem("gdn_l"), pe.next("gdn_l"))
                    if pe.reused("gdn_tr", 4):
                        eng.wait_ge(sem("gdn_tr"), pe.freed("gdn_tr", 4))
                    eng.transpose(ps[:, 0:P], MT[:, b, :], C("ident"))
                    eng.transpose(ps[:, P:S], qk_t[:, b, :], C("ident")).then_inc(sem("gdn_tr_mm"), 1)
                eng.wait_ge(sem("gdn_tr"), pe.uses["gdn_tr"])
                eng.wait_ge(sem("gdn_tok"), pe.uses["gdn_tok"])
                inverse(8)
                for b in range(8):
                    ps = PB[b % 4]
                    if pe.reused("uw_ev", 4):
                        eng.wait_ge(sem("uw_ev"), pe.freed("uw_ev", 4))
                    eng.matmul(ps[:, 0:P], INV[:, b, :], vb_t[:, b, :], start=True, stop=True)
                    eng.matmul(ps[:, P:S], kb_t[:, b, :], INV[:, b, :], start=True, stop=True).then_inc(sem("uw_mm"), 1)
                eng.wait_ge(sem("uw_ev"), pe.uses["uw_ev"])
                for c in range(4):
                    tt, r = c // 2, slice(CH * (c % 2), CH * (c % 2) + CH)
                    q = slice(CH * c, CH * c + CH)
                    eng.wait_ge(sem("gstate_up"), pe.next("gstate_up"))
                    for h in range(4):
                        ins = eng.matmul(PB[0][r, h * P:h * P + P], w_t[:, 2 * h + tt, r], GS[:, h, :],
                                         start=True, stop=True)
                    ins.then_inc(sem("gv_mm"), 1)
                    eng.wait_ge(sem("gv_ev"), pe.next("gv_ev"))
                    if pe.reused("go_ev", 1):
                        eng.wait_ge(sem("go_ev"), pe.freed("go_ev", 1))
                    for h in range(4):
                        b = 2 * h + tt
                        eng.matmul(PB[1][:, h * CH:h * CH + CH], GS[:, h, :], gq[:, h, q], start=True, stop=False)
                        ins = eng.matmul(PB[1][:, h * CH:h * CH + CH], vn_t[:, h, :], qk2_t[:, b, r],
                                         start=False, stop=True)
                    if c < 3:
                        for h in range(4):
                            ins = eng.matmul(PB[2][:, h * P:h * P + P], kd_t[r, 2 * h + tt, :], vn_t[r, h, :],
                                             start=True, stop=True)
                    ins.then_inc(sem("gstate_mm"), 1)
                eng.wait_ge(sem("go_ev"), pe.uses["go_ev"])
                eng.wait_ge(sem("go_sq"), pe.next("go_sq"))
                for h in range(4):
                    ins = eng.matmul(PB[4 + h // 2][:, (h % 2) * S:(h % 2) * S + S], C("ones"), gsq[:, h, :],
                                     start=True, stop=True)
                ins.then_inc(sem("go_mm"), 1)

            start_up()
            for l in range(DEPTH):
                norm_sum(square, KD)
                eng.wait_ge(sem("h_ready"), pe.next("h_ready"))
                for label in first_tiles(l):
                    project(label)
                rope(att_rope(l) + ret_rope(l), later_tiles(l)[:ROPE_FILL])
                rope_finished()
                indexer(l)
                attention(dsa_jobs(), attention_fill(l))
                retention(l)
                eng.wait_ge(sem("pooled"), pe.next("pooled"))
                for j in range(4):
                    stream(("pool", l, j), lambda i: pooled[:, j, :])
                rwkv(l)
                eng.wait_ge(sem("oD_ready"), pe.next("oD_ready"))
                eng.wait_ge(sem("oB_ready"), pe.next("oB_ready"))
                for m in range(KD):
                    for b in range(4):
                        stream(("gate", l, m, b), hidden)
                        stream(("branch", l, m, b), lambda i: branch_out[b][:, i, :])
                eng.wait_ge(sem("merged"), pe.next("merged"))
                for m in range(KD):
                    stream(("wout", l, m), lambda i: merged[:, i, :])
                norm_sum(square, KD)
                eng.wait_ge(sem("h_ready"), pe.next("h_ready"))
                for j in range(DFF // P):
                    stream(("up", l, j), hidden)
                eng.wait_ge(sem("up_ready"), pe.next("up_ready"))
                for m in range(KD):
                    stream(("down", l, m), lambda i: up_t[:, i, :])
            norm_sum(square, KD)
            for l in range(DEPTH):
                norm_sum(square, KD)
                eng.wait_ge(sem("h_ready"), pe.next("h_ready"))
                if l == 0:
                    for j in range(12):
                        stream(("conv", j), hidden)
                    stream(("ba",), hidden, tokens=True)
                    for j in range(4):
                        stream(("z", j), hidden)
                    for name in ("mq", "mk"):
                        for j in range(4):
                            stream((name, j), hidden)
                    for j in range(4):
                        stream(("mv", j), hidden, tokens=True)
                    rope(moba_rope())
                    rope_finished()
                    gdn(l)
                    eng.wait_ge(sem("evac"), tiles[("mv", 3)][0] + 1)
                    attention(moba_jobs())
                else:
                    for j in range(6):
                        stream(("c", j), hidden)
                    stream(("kr",), hidden)
                    norm_sum(lat_sq[:, 0:4, :], 4)
                    norm_sum(lat_sq[:, 4:6, :], 2)
                    eng.wait_ge(sem("lat_ready"), pe.next("lat_ready"))
                    for h in range(8):
                        stream(("qn", h), lambda i: lat[:, i, :])
                    for j in range(4):
                        stream(("qr", j), lambda i: lat[:, i, :])
                    for h in range(8):
                        stream(("kn", h), lambda i: lat[:, 4 + i, :])
                    for h in range(8):
                        stream(("lv", h), lambda i: lat[:, 4 + i, :], tokens=True)
                    rope(mla_rope())
                    rope_finished()
                    eng.wait_ge(sem("kr_ready"), pe.next("kr_ready"))
                    eng.wait_ge(sem("evac"), tiles[("lv", 7)][0] + 1)
                    attention(mla_jobs())
                if l == 0:
                    eng.wait_ge(sem("gdn_ready"), pe.next("gdn_ready"))
                for m in range(KD):
                    stream(("mix", l, m), lambda i: mix_t[:, i, :])
                norm_sum(square, KD)
                eng.wait_ge(sem("h_ready"), pe.next("h_ready"))
                experts(l)
                gate_matrices(l)
                expert_tiles(l)
            norm_sum(square, KD)
            eng.wait_ge(sem("h_ready"), pe.next("h_ready"))
            for tt in range(TT):
                for k in range(KD):
                    ins = eng.transpose(PB[2 * tt + k // 4][:, (k % 4) * P:(k % 4) * P + P],
                                        hT[:, k, tt * P:tt * P + P], C("ident"))
            ins.then_inc(sem("out_mm"), 1)

        @block.scalar
        def _(eng):
            act = Counts()
            copied = [0]

            def evac(label, dest, func=ACT.Copy, **kw):
                t, _, _, n = tiles[label]
                assert t == copied[0], (label, t, copied[0])
                copied[0] += 1
                eng.wait_ge(sem("unit_done"), last_unit(label))
                src = PB[t % BANKS][0:n, 0:S]
                if len(dest.shape) == 3:
                    n = dest.shape[2]
                    src = PB[t % BANKS][:, 0:S].rearrange("p (a b) -> p a b", b=P)[:, :, 0:n]
                if dest.shape[-1] == 1:
                    src = PB[t % BANKS][:, 0:1]
                if dest.shape[-1] == 512:
                    src = PB[t % BANKS][:, :]
                eng.activation(dest, src, func, **kw).then_inc(sem("evac"), 1)

            def square_of(x, sq):
                eng.activation(sq, x, ACT.Square).then_inc(sem("sq_ready"), 1)

            def root(x):
                eng.wait_ge(sem("root_in"), act.next("root_in"))
                eng.activation(x, x, ACT.Sqrt).then_inc(sem("root_out"), 1)

            def residual_ready():
                if act.uses["res_add"] > 0:
                    eng.wait_ge(sem("res_add"), act.uses["res_add"])

            def sines():
                for i in range(2):
                    eng.wait_ge(sem("angles"), act.next("angles"))
                    eng.activation(tab[:, i, 0, :], tab[:, i, 1, :], ACT.Sin, scale=0.5).then_inc(sem("act_step"), 1)
                    eng.wait_ge(sem("act_step"), act.next("act_step"))
                    eng.activation(tab[:, i, 1, :], tab[:, i, 1, :], ACT.Sin).then_inc(sem("sines"), 1)

            def projected(label):
                if label[0] != "mod":
                    evac(label, place_of(label), ACT.Silu if label[0] == "rg" else ACT.Copy)

            def attention(jobs, fill=()):
                def exps(j):
                    eng.wait_ge(sem("sm_ready"), act.next("sm_ready"))
                    ns = jobs[j]["ns"]
                    eng.activation(probs[:, j % 2, 0:ns], probs[:, j % 2, 0:ns], ACT.Exp, bias=nmx[:, j % 2:j % 2 + 1],
                                   accum_out=den[:, j % 2:j % 2 + 1]).then_inc(sem("exp_ready"), 1)

                def outputs(j):
                    job = jobs[j]
                    eng.wait_ge(sem("pT_mm"), act.next("pT_mm"))
                    if act.reused("pv_mm", 2):
                        eng.wait_ge(sem("pv_mm"), act.freed("pv_mm", 2))
                    eng.activation(probsT[:, j % 2, 0:job["ns"]], PB[4 + j % 2][:, 0:job["ns"]],
                                   ACT.Copy).then_inc(sem("pT_ready"), 1)
                    eng.wait_ge(sem("pv_mm"), act.next("pv_mm"))
                    eng.activation(job["dest"], PB[4 + j % 2][job["rows"], 256:384],
                                   ACT.Copy).then_inc(sem("pv_out"), 1)

                exps(0)
                for j in range(len(jobs)):
                    if j + 1 < len(jobs):
                        exps(j + 1)
                    for label in fill[j] if fill else ():
                        projected(label)
                    outputs(j)

            def inverse(blocks):
                for n in range(5):
                    for g in range(blocks // 4):
                        eng.wait_ge(sem("sq_mm"), act.next("sq_mm"))
                        if n < 4:
                            eng.activation(MS[:, 4 * g:4 * g + 4, :].rearrange("p a b -> p (a b)"), PB[4 * g][:, :],
                                           ACT.Copy).then_inc(sem("sq_ev"), 1)

            def rwkv(l):
                eng.wait_ge(sem("shifted"), act.next("shifted", 3))
                eng.activation(shifted["wd"][0:32, 0, :], shifted["wd"][0:32, 0, :], ACT.Tanh)
                eng.activation(shifted["gd"][0:96, 0, :], shifted["gd"][0:96, 0, :], ACT.Sigmoid).then_inc(
                    sem("lora_in"), 1)
                act.seen["shifted"] += 3
                for j in range(4):
                    evac(("w2", l, j), LD[:, j, :], ACT.Sigmoid, bias=vcol(l, VEC1, "rwkv_w0", j))
                for j in range(4):
                    evac(("a2", l, j), RA[:, j, :], ACT.Sigmoid, bias=vcol(l, VEC1, "rwkv_a0", j))
                for j in range(4):
                    evac(("g2", l, j), RG[:, j, :])
                eng.wait_ge(sem("kk_sum"), act.next("kk_sum"))
                for b in range(2):
                    ins = eng.activation(EX[:, 2 * b:2 * b + 2, :].rearrange("p a b -> p (a b)"), PB[4 + b][:, :], ACT.Sqrt)
                ins.then_inc(sem("kk_root"), 1)
                eng.wait_ge(sem("log_decays"), act.next("log_decays"))
                eng.activation(EP, RL, ACT.Exp)
                eng.activation(EN, RL, ACT.Exp, scale=-1.0)
                eng.activation(EX, EX, ACT.Exp).then_inc(sem("decays"), 1)
                for half in range(2):
                    for b in range(8):
                        eng.wait_ge(sem("block_mm"), act.next("block_mm"))
                        eng.activation(TOK[:, b, :, :].rearrange("p a b -> p (a b)"), PB[4 * (b % 2) + 3][:, 0:384],
                                       ACT.Copy).then_inc(sem("tok_ev"), 1)
                    inverse(8)
                    for c in range(2):
                        eng.wait_ge(sem("u_mm"), act.next("u_mm"))
                        eng.activation(US.rearrange("p a b -> p (a b)"), PB[1][:, :], ACT.Copy).then_inc(sem("u_ev"), 1)
                        eng.wait_ge(sem("state_mm"), act.next("state_mm"))
                        t0 = CH * (2 * half + c)
                        y = PB[2][:, :].rearrange("p (a b) -> p a b", b=P)
                        for s in range(2):
                            r = slice(CH * s, CH * s + CH)
                            ins = eng.activation(YT[r, :, t0:t0 + CH], y[r, :, CH * s:CH * s + CH], ACT.Copy)
                        ins.then_inc(sem("y_ev"), 1)
                root(gn_rs)

            def merge(l):
                for m in range(KD):
                    for b in range(4):
                        if act.reused("gated", 4):
                            eng.wait_ge(sem("gated"), act.freed("gated", 4))
                        evac(("gate", l, m, b), gate_s[:, b, :], ACT.Sigmoid, bias=vcol(l, VEC1, "gate_b", 8 * b + m))
                        evac(("branch", l, m, b), proj_s[:, b, :])

            def to_residual(name, l, buf):
                for m in range(KD):
                    if act.reused("res_add", 4):
                        eng.wait_ge(sem("res_add"), act.freed("res_add", 4))
                    evac((name, l, m), buf[:, m % 4, :])

            def gdn():
                for j in range(12):
                    eng.wait_ge(sem("conv_done"), act.next("conv_done"))
                    ins = eng.activation(gqkv[:, j, :], gqkv[:, j, :], ACT.Silu)
                    if j == 7:
                        ins.then_inc(sem("act_step"), 1)
                        eng.wait_ge(sem("act_step"), act.next("act_step"))
                        eng.activation(gsq, gqkv[:, 0:8, :], ACT.Square).then_inc(sem("gdn_sq"), 1)
                ins.then_inc(sem("act_step"), 1)
                eng.wait_ge(sem("act_step"), act.next("act_step"))
                eng.activation(beta_t, ba_t[:, :, 0:4], ACT.Sigmoid)
                eng.wait_ge(sem("sp_x"), act.next("sp_x"))
                eng.activation(sp_t[:, 1, :, :], sp_t[:, 1, :, :], ACT.Exp, scale=-1.0).then_inc(sem("act_step"), 1)
                eng.wait_ge(sem("act_step"), act.next("act_step"))
                eng.activation(sp_t[:, 1, :, :], sp_t[:, 1, :, :], ACT.Ln, bias=1.0)
                eng.activation(ab_t[:, 0, 0:4], ab_t[:, 0, 0:4], ACT.Exp).then_inc(sem("sp_ln"), 1)
                root(gsq)
                eng.wait_ge(sem("gdn_cum"), act.next("gdn_cum"))
                eng.activation(eg_t[:, 0, :, :], eg_t[:, 0, :, :], ACT.Exp)
                eng.activation(eg_t[:, 1, :, :], eg_t[:, 1, :, :], ACT.Exp).then_inc(sem("eg_ready"), 1)
                eng.wait_ge(sem("grow_mm"), act.next("grow_mm"))
                for i in range(2):
                    ins = eng.activation(erow[:, 2 * i:2 * i + 2, :].rearrange("p a b -> p (a b)"), PB[6 + i][:, :], ACT.Exp)
                ins.then_inc(sem("erow_ready"), 1)
                eng.wait_ge(sem("dmat_in"), act.next("dmat_in"))
                eng.activation(dmat, dmat, ACT.Exp, scale=-1.0).then_inc(sem("dmat_ready"), 1)
                inverse(8)
                for b in range(8):
                    eng.wait_ge(sem("uw_mm"), act.next("uw_mm"))
                    eng.activation(uw_t[:, b, :], PB[b % 4][:, 0:S], ACT.Copy).then_inc(sem("uw_ev"), 1)
                for c in range(4):
                    eng.wait_ge(sem("gstate_mm"), act.next("gstate_mm"))
                    ins = eng.activation(mix_t[:, 0:4, CH * c:CH * c + CH],
                                         PB[1][:, 0:S].rearrange("p (a b) -> p a b", b=CH), ACT.Copy)
                    ins.then_inc(sem("go_ev"), 1)
                    eng.wait_ge(sem("go_ev"), act.next("go_ev"))
                eng.activation(gsq[:, 0:4, :], mix_t[:, 0:4, :], ACT.Square).then_inc(sem("go_sq"), 1)
                root(gsq[:, 0:4, :])

            def experts(l):
                for j in range(16):
                    evac(("pq", l, j), pq_t[:, j, :])
                for j in range(4):
                    evac(("sub", l, j), sub_t[:, 4 * j:4 * j + 4, :].rearrange("p a b -> p (a b)"))
                for tt in range(TT):
                    for b in range(4):
                        eng.wait_ge(sem("key_mm"), act.next("key_mm"))
                        eng.activation(key_t[:, tt, 4 * b:4 * b + 4, :].rearrange("p a b -> p (a b)"), PB[4 + b][:, :],
                                       ACT.Copy).then_inc(sem("key_ev"), 1)
                eng.wait_ge(sem("gate_logits"), act.next("gate_logits"))
                eng.activation(cv, cv, ACT.Exp).then_inc(sem("gate_exp"), 1)
                eng.wait_ge(sem("pickT_mm"), act.next("pickT_mm"))
                for i in range(3):
                    ins = eng.activation(selT[:, i, :], PB[4 + i][:, 0:S], ACT.Copy)
                ins.then_inc(sem("pickT_ev"), 1)

            def gate_matrices(l):
                base = 64 * l
                with eng.Fori(0, 32) as i:
                    for b in range(2):
                        if positive(i * 2 + (b + 1 + base)):
                            eng.wait_ge(sem("gate_mm"), i * 2 + (b + 1 + base))
                        eng.activation(arena[:, bass.ds(i * 1024 + b * 512, 512)], PB[b][:, :],
                                       ACT.Copy).then_inc(sem("gate_ev"), 1)

            def expert_tiles(l):
                base = NKEY * l

                def u_high(e):
                    if positive(e + base):
                        eng.wait_ge(sem("exp_mm"), e + base)
                    for q in range(2):
                        d = slice(q * 512, q * 512 + 512)
                        eng.wait_ge(sem("u_turned"), e * 2 + (2 * base + q + 1))
                        eng.activation(u_parts[:, 0, d], PB[4 + q][:, :], ACT.Copy).then_inc(sem("uH_ready"), 1)

                def activate(e, j):
                    b = j % 2
                    eng.wait_ge(sem("exp_mm"), e + (1 + base))
                    if positive(e + (base - 1)):
                        eng.wait_ge(sem("v_free"), e + (base - 1))
                    eng.activation(gelu[:, b, :], PB[6 + b][:, 0:S], ACT.Gelu).then_inc(sem("gelu_done"), 1)
                    eng.wait_ge(sem("weighed"), e + (1 + base))
                    eng.activation(w_high[:, b, :], gelu[:, b, :], ACT.Copy).then_inc(sem("wH_ready"), 1)
                    n = 16 * (e // 4 + 1) + 512 * l if isinstance(e, int) else e * 4 + (16 + 512 * l - 4 * j)
                    eng.wait_ge(sem(f"v_full{j}"), n)
                    if positive(e + base):
                        eng.wait_ge(sem("v_free"), e + base)
                    eng.activation(v_high, ring[:, 2 + j, :], ACT.Copy).then_inc(sem("vH_ready"), 1)

                eng.wait_ge(sem("unit_done"), last_unit(("sub", l, 3)))
                eng.activation(h_high, hT, ACT.Copy).then_inc(sem("hH_ready"), 1)
                u_high(0)
                for e in range(4):
                    u_high(e + 1)
                    activate(e, e)
                with eng.Fori(1, 31) as i:
                    for j in range(4):
                        u_high(i * 4 + (j + 1))
                        activate(i * 4 + j, j)
                for j in range(4):
                    if j < 3:
                        u_high(125 + j)
                    activate(124 + j, j)
                eng.wait_ge(sem("v_free"), base + NKEY)
                for q in range(2):
                    ins = eng.activation(moe_t[:, 0, q * 512:q * 512 + 512], PB[q][:, :], ACT.Copy)
                ins.then_inc(sem("experts0_ev"), 1)

            eng.wait_ge(sem("setup_mm"), act.next("setup_mm"))
            eng.activation(vec[:, :, :].rearrange("p a b -> p (a b)"), PB[0][:, :], ACT.Copy).then_inc(sem("vec_ready"), 1)
            for b in range(4):
                ins = eng.activation(xT[:, 2 * b:2 * b + 2, :].rearrange("p a b -> p (a b)"), PB[1 + b][:, :], ACT.Copy)
            ins.then_inc(sem("x_ready"), 1)
            eng.wait_ge(sem("x_ready"), act.next("x_ready"))
            eng.wait_ge(sem("vec_ready"), act.next("vec_ready"))
            eng.activation(cond, vec[:, 3, VEC3["c"][0]:VEC3["c"][0] + 8], ACT.Silu).then_inc(sem("cond_ready"), 1)
            sines()
            for l in range(DEPTH):
                residual_ready()
                square_of(xT[:, :, :], square)
                root(rstd)
                for label in first_tiles(l) + later_tiles(l)[:INDEXER_END]:
                    projected(label)
                attention(dsa_jobs(), attention_fill(l))
                for h in range(8):
                    r = slice(64 * (h % 2), 64 * (h % 2) + 64)
                    eng.wait_ge(sem("ret_out_mm"), act.next("ret_out_mm"))
                    eng.activation(oD[r, h // 2, :], PB[4 + h % 2][r, 0:S], ACT.Copy).then_inc(sem("ret_out_ev"), 1)
                eng.wait_ge(sem("unit_done"), mod_unit[l, MOD - 1] + 1)
                eng.activation(mod_rows, PB[3][0:MOD, 0:P], ACT.Copy).then_inc(sem("mod_rows"), 1)
                root(gn_rs)
                for j in range(4):
                    evac(("pool", l, j), oC[:, j, :], ACT.Copy, scale=vcol(l, VEC1, "pool_scale", j))
                rwkv(l)
                merge(l)
                to_residual("wout", l, res_s)
                residual_ready()
                square_of(xT[:, :, :], square)
                root(rstd)
                for j in range(DFF // P):
                    evac(("up", l, j), up_t[:, j, :], ACT.Relu)
                    eng.wait_ge(sem("evac"), tiles[("up", l, j)][0] + 1)
                    ins = eng.activation(up_t[:, j, :], up_t[:, j, :], ACT.Square)
                ins.then_inc(sem("up_ready"), 1)
                to_residual("down", l, res_s)
            residual_ready()
            square_of(xT[:, :, :], square)
            root(rstd)
            sines()
            for l in range(DEPTH):
                eng.wait_ge(sem("x_ready"), act.next("x_ready"))
                square_of(xT[:, :, :], square)
                root(rstd)
                if l == 0:
                    for j in range(12):
                        evac(("conv", j), conv_in[:, j, 3:3 + S])
                    evac(("ba",), ba_t)
                    for j in range(4):
                        evac(("z", j), z_t[:, j, :], ACT.Silu)
                    for name, t in (("mq", mq_t), ("mk", mk_t)):
                        for j in range(4):
                            evac((name, j), t[:, j, :])
                    for j in range(4):
                        evac(("mv", j), mv_t[:, j, :, :])
                    gdn()
                    attention(moba_jobs())
                else:
                    for j in range(6):
                        evac(("c", j), lat[:, j, :])
                    eng.wait_ge(sem("evac"), tiles[("c", 5)][0] + 1)
                    square_of(lat[:, 0:4, :], lat_sq[:, 0:4, :])
                    square_of(lat[:, 4:6, :], lat_sq[:, 4:6, :])
                    root(rstd)
                    root(rstd)
                    evac(("kr",), kr_t[:, 0, :])
                    for h in range(8):
                        evac(("qn", h), qn_t[:, h, :])
                    for j in range(4):
                        evac(("qr", j), qr_t[:, j, :])
                    for h in range(8):
                        evac(("kn", h), kn_t[:, h, :])
                    for h in range(8):
                        evac(("lv", h), lv_t[:, h, :, :])
                    attention(mla_jobs())
                to_residual("mix", l, res2_s)
                residual_ready()
                square_of(xT[:, :, :], square)
                root(rstd)
                experts(l)
                gate_matrices(l)
                expert_tiles(l)
            eng.wait_ge(sem("x_ready"), act.next("x_ready"))
            square_of(xT[:, :, :], square)
            root(rstd)
            eng.wait_ge(sem("out_mm"), act.next("out_mm"))
            for i in range(4):
                ins = eng.activation(out_t[:, i // 2, (i % 2) * 512:(i % 2) * 512 + 512], PB[i][:, :], ACT.Copy)
            ins.then_inc(sem("out_ready"), 1)

        @block.gpsimd
        def _(eng):
            pool = Counts()
            tt_, ts_ = eng.tensor_tensor, eng.tensor_scalar

            def copied_out(label):
                eng.wait_ge(sem("evac"), tiles[label][0] + 1)

            def means(l):
                n = S + 16
                for g in range(4):
                    copied_out(("pc", l, g))
                    src = pc_t[:, g, :]
                    for k in range(g + 1):
                        dst = (pool_a, pool_b)[k % 2][:, 0, :]
                        lo, d = 2 ** (k + 1) - 1, 2 ** k
                        tt_(dst[:, lo:n], src[:, lo:n], src[:, lo - d:n - d], ALU.add).then_inc(sem("pool_step"), 1)
                        eng.wait_ge(sem("pool_step"), pool.next("pool_step"))
                        src = dst
                    x = pc_t[:, g, 16:n]
                    ts_(pooled[:, g, :], src[:, 16:n], 2.0 ** -(g + 1), None, ALU.mult).then_inc(sem("pool_step"), 1)
                    eng.wait_ge(sem("pool_step"), pool.next("pool_step"))
                    tt_(pooled[:, g, :], pooled[:, g, :], x, ALU.subtract).then_inc(sem("pool_step"), 1)
                    eng.wait_ge(sem("pool_step"), pool.next("pool_step"))
                    first = C("pool_first")[:, 16 * g:16 * g + 16]
                    tt_(pooled[:, g, 0:16], src[:, 16:32], first, ALU.mult).then_inc(sem("pool_step"), 1)
                    eng.wait_ge(sem("pool_step"), pool.next("pool_step"))
                    ins = tt_(pooled[:, g, 0:16], pooled[:, g, 0:16], x[:, 0:16], ALU.subtract)
                    done = "pooled" if g == 3 else "pool_step"
                    ins.then_inc(sem(done), 1)
                    eng.wait_ge(sem(done), pool.next(done))

            def shift(l):
                for name, _, n in SHIFTED:
                    t, m = -(-n // P), min(P, n)
                    copied_out(("s" + name, l, t - 1))
                    now, before, to = raw[name][0:m, :, 1:S + 1], raw[name][0:m, :, 0:S], shifted[name][0:m]
                    tt_(to, before, now, ALU.subtract).then_inc(sem("pool_step"), 1)
                    eng.wait_ge(sem("pool_step"), pool.next("pool_step"))
                    for j in range(t):
                        ins = ts_(to[:, j, :], to[:, j, :], vcol(l, VEC1, "mu_" + name, j)[0:m], None, ALU.mult)
                    ins.then_inc(sem("pool_step"), 1)
                    eng.wait_ge(sem("pool_step"), pool.next("pool_step"))
                    tt_(to, to, now, ALU.add).then_inc(sem("shifted"), 1)
                    eng.wait_ge(sem("shifted"), pool.next("shifted"))
            for l in range(DEPTH):
                eng.wait_ge(sem("h_ready"), 2 * l + 1)
                eng.dma_start(decay_t, io["decay"].rearrange("p (a b) -> p a b", b=384)).then_inc(sem("decay_in"), 16)
                for t in [pc_t[:, :, 0:16]] + [raw[name][:, :, 0:1] for name in raw]:
                    ins = eng.memset(t, 0.0)
                eng.memset(cond_at, 0.0).then_inc(sem("pool_step"), 1)
                eng.wait_ge(sem("pool_step"), pool.next("pool_step"))
                eng.wait_ge(sem("cond_ready"), 1)
                eng.tensor_copy(cond_at[:, :, MOD - 1:MOD], cond.unsqueeze(2)).then_inc(sem("cond_placed"), 1)
                means(l)
                shift(l)
            eng.wait_ge(sem("h_ready"), 5)
            for i, name in enumerate(("gdn_a_log_2", "gdn_dt_bias_2")):
                eng.dma_start(ab_t[:, 0, 4 * i:4 * i + 4], io[name].to_broadcast([P, 4])).then_inc(sem("ab_in"), 16)

        @block.sync
        def _(eng):
            sp = Counts()

            def setup(dst, src):
                eng.dma_start(dst, src).then_inc(sem("setup_in"), 16)

            def vector_rows(i, spec, name, src):
                at, n = spec[name]
                setup(rows_in[at:at + n, i, 0:src.shape[-1]], src)

            def matrix(src):
                return src.rearrange("(a b) -> a b", b=P)

            loaded = [0]

            def load_units(end):
                for n in range(loaded[0], end):
                    if n - RING + 1 > 0:
                        eng.wait_ge(sem("unit_done"), n - RING + 1)
                    for rows, k, at, width, src, total in units[n]:
                        eng.dma_start(slot_view(n, rows, k, total)[:, :, at:at + width], src).then_inc(
                            sem(f"w_full{n % RING}"), 16)
                loaded[0] = max(loaded[0], end)

            def load_experts(l):
                def pair(e, j):
                    rows = slice(e * P, e * P + P) if isinstance(e, int) else bass.ds(e * P, P)
                    if positive(e * 2 + (2 * NKEY * l - 2)):
                        eng.wait_ge(sem("u_turned"), e * 2 + (2 * NKEY * l - 2))
                    eng.dma_start(ring[:, j % 2, :], io["peer_u_2"][l][rows, :]).then_inc(sem(f"u_full{j % 2}"), 16)
                    if positive(e + (NKEY * l - 3)):
                        eng.wait_ge(sem("v_free"), e + (NKEY * l - 3))
                    eng.dma_start(ring[:, 2 + j, :], io["peer_v_2"][l][rows, :]).then_inc(sem(f"v_full{j}"), 16)

                eng.wait_ge(sem("unit_done"), loaded[0])
                for e in range(4):
                    pair(e, e)
                with eng.Fori(1, 32) as i:
                    for j in range(4):
                        pair(i * 4 + j, j)
                eng.wait_ge(sem("u_turned"), 2 * NKEY * (l + 1))
                eng.wait_ge(sem("v_free"), NKEY * (l + 1))

            setup(cst[:, :], io["consts"])
            setup(x_in, io["x"][0].rearrange("(a p) d -> p a d", p=P))
            for i, name in enumerate(("positions", "positions_2")):
                setup(ipos[:, i, :], io[name].to_broadcast([P, S]))
            eng.wait_ge(sem("rows_zero"), 1)
            for l in range(DEPTH):
                for name in ("attn_norm_g", "mlp_norm_g", "rwkv_w0", "rwkv_a0", "rwkv_k_k", "rwkv_k_a", "rwkv_r_k",
                             "rwkv_ln_g", "rwkv_ln_b", "pool_scale", "ret_gn_g"):
                    vector_rows(l, VEC1, name, matrix(io[name][l]))
                vector_rows(l, VEC1, "gate_b", io["gate_b"][l].rearrange("g (a b) -> (g a) b", b=P))
                for name, c0, n in SHIFTED:
                    src = io["rwkv_mu"][l:l + 1, c0:c0 + n]
                    vector_rows(l, VEC1, "mu_" + name, src if n < P else matrix(io["rwkv_mu"][l, c0:c0 + n]))
                for name in ("norm_mix", "norm_ffn", "mod_b"):
                    vector_rows(2, VEC2, f"{name}{l}", matrix(io[name + "_2"][l]))
            vector_rows(3, VEC3, "conv", io["gdn_conv_2"][0].rearrange("j (a b) -> (j a) b", b=P))
            vector_rows(3, VEC3, "gdn_o_norm", io["gdn_o_norm_2"])
            for name in ("mla_q_norm", "mla_kv_norm"):
                vector_rows(3, VEC3, name, matrix(io[name + "_2"][0]))
            for name in ("final_norm_g", "final_norm_2"):
                vector_rows(3, VEC3, name, matrix(io[name]))
            vector_rows(3, VEC3, "c", matrix(io["c_2"][0]))
            for l in range(DEPTH):
                load_units(stage_units[25 + 10 * l])
                load_experts(l)
            eng.wait_ge(sem("out_ready"), sp.next("out_ready"))
            eng.dma_start(out[0].rearrange("(a p) d -> p a d", p=P), out_t).then_inc(sem("stored"), 16)
            eng.wait_ge(sem("stored"), 16)

        @block.vector
        def _(eng):
            dve = Counts()
            tt_, ts_, stt_ = eng.tensor_tensor, eng.tensor_scalar, eng.scalar_tensor_tensor

            def copied_out(label):
                eng.wait_ge(sem("evac"), tiles[label][0] + 1)

            def angles(slot, kind, col, pos):
                two_pi = 2 * np.pi
                c1 = 6.28125
                c2 = np.floor((two_pi - c1) * 2 ** 20) / 2 ** 20
                c3 = two_pi - c1 - c2
                magic = 1.5 * 2 ** 23
                freq = cst[:, CONST_AT["freq"][0] + col:CONST_AT["freq"][0] + col + 1]
                ang, turns = angle_t[:, 0, :], angle_t[:, 1, :]
                ts_(ang, wT[:, pos, :], freq, None, ALU.mult).then_inc(sem("dve_step"), 1)
                eng.wait_ge(sem("dve_step"), dve.next("dve_step"))
                ts_(turns, ang, 1 / two_pi, magic, ALU.mult, ALU.add).then_inc(sem("dve_step"), 1)
                eng.wait_ge(sem("dve_step"), dve.next("dve_step"))
                ts_(turns, turns, -magic, None, ALU.add).then_inc(sem("dve_step"), 1)
                eng.wait_ge(sem("dve_step"), dve.next("dve_step"))
                for c in (c1, c2, c3):
                    stt_(ang, turns, -float(c), ang, ALU.mult, ALU.add).then_inc(sem("dve_step"), 1)
                    eng.wait_ge(sem("dve_step"), dve.next("dve_step"))
                ts_(tab[:, slot, 1, :], ang, 3.1415925, -3.1415925, ALU.min, ALU.max).then_inc(sem("angles"), 1)
                eng.wait_ge(sem("angles"), dve.next("angles"))

            def cosine(slot):
                eng.wait_ge(sem("sines"), dve.next("sines"))
                tt_(tab[:, slot, 0, :], tab[:, slot, 0, :], tab[:, slot, 0, :], ALU.mult).then_inc(sem("dve_step"), 1)
                eng.wait_ge(sem("dve_step"), dve.next("dve_step"))
                ts_(tab[:, slot, 0, :], tab[:, slot, 0, :], -2.0, 1.0, ALU.mult, ALU.add).then_inc(sem("dve_step"), 1)
                eng.wait_ge(sem("dve_step"), dve.next("dve_step"))

            def root(x):
                eng.reciprocal(x, x).then_inc(sem("root_in"), 1)
                eng.wait_ge(sem("root_in"), dve.next("root_in"))
                eng.wait_ge(sem("root_out"), dve.next("root_out"))

            def inv_norm(n, eps):
                eng.wait_ge(sem("ss_ready"), dve.next("ss_ready"))
                ts_(rstd, PB[4][:, 0:S], 1.0 / n, eps, ALU.mult, ALU.add).then_inc(sem("ss_read"), 1)
                eng.wait_ge(sem("ss_read"), dve.next("ss_read"))
                root(rstd)

            def scaled(dst, gains):
                for k in range(KD):
                    ins = stt_(dst[:, k, :], xT[:, k, :], gains[:, k:k + 1], rstd, ALU.mult, ALU.mult)
                return ins

            def norm(dst, gains, eps=1e-5):
                inv_norm(D, eps)
                return scaled(dst, gains)

            def modulated_norm(l, which):
                rows = VEC2[("norm_mix", "norm_ffn")[which] + str(l)][0]
                shift, scale = mod[:, l, 24 * which:24 * which + 8], mod[:, l, 24 * which + 8:24 * which + 16]
                inv_norm(D, 1e-6)
                gm = small[:, 24:32]
                stt_(gm, scale, 1.0, vec[:, 2, rows:rows + 8], ALU.add, ALU.mult).then_inc(sem("dve_step"), 1)
                eng.wait_ge(sem("dve_step"), dve.next("dve_step"))
                scaled(hT, gm).then_inc(sem("dve_step"), 1)
                eng.wait_ge(sem("dve_step"), dve.next("dve_step"))
                for k in range(KD):
                    ins = ts_(hT[:, k, :], hT[:, k, :], shift[:, k:k + 1], None, ALU.add)
                ins.then_inc(sem("h_ready"), 1)
                eng.wait_ge(sem("h_ready"), dve.next("h_ready"))

            def rope(what, slot):
                for ap, _, _ in what:
                    j = dve.uses["rope"] % 2
                    dve.uses["rope"] += 1
                    eng.wait_ge(sem("rot_mm"), dve.next("rot_mm"))
                    tt_(rope_tmp[:, j, :], PB[4 + j][:, 0:S], tab[:, slot, 1, :], ALU.mult).then_inc(sem("dve_step"), 1)
                    eng.wait_ge(sem("dve_step"), dve.next("dve_step"))
                    tt_(ap, ap, tab[:, slot, 0, :], ALU.mult).then_inc(sem("dve_step"), 1)
                    eng.wait_ge(sem("dve_step"), dve.next("dve_step"))
                    tt_(ap, ap, rope_tmp[:, j, :], ALU.add).then_inc(sem("rope_done"), 1)
                    eng.wait_ge(sem("rope_done"), dve.next("rope_done"))

            def indexer(l):
                copied_out(("wi", l))
                a, w = idx[:, 0, :], work[:, 0, :]
                for i in range(TT):
                    ns, dg = P * (i + 1), slice(P * i, P * i + P)
                    eng.wait_ge(sem("idx_mm"), dve.next("idx_mm"))
                    for h in range(4):
                        ps = PB[6 + h % 2][:, (h // 2) * S:(h // 2) * S + ns]
                        done = "idx_done" if h == 3 else "dve_step"
                        ts_((w if h else a)[:, 0:ns], ps, 0.0, wi_t[:, i, h:h + 1], ALU.max, ALU.mult).then_inc(sem(done), 1)
                        eng.wait_ge(sem(done), dve.next(done))
                        if h:
                            tt_(a[:, 0:ns], a[:, 0:ns], w[:, 0:ns], ALU.add).then_inc(sem("dve_step"), 1)
                            eng.wait_ge(sem("dve_step"), dve.next("dve_step"))
                    tt_(a[:, dg], a[:, dg], C("tri01"), ALU.mult).then_inc(sem("dve_step"), 1)
                    eng.wait_ge(sem("dve_step"), dve.next("dve_step"))
                    tt_(a[:, dg], a[:, dg], C("tri_fill"), ALU.add).then_inc(sem("dve_step"), 1)
                    eng.wait_ge(sem("dve_step"), dve.next("dve_step"))
                    src = a
                    for n in range(TOPK // 8):
                        eng.max(m8, src[:, 0:ns]).then_inc(sem("dve_step"), 1)
                        eng.wait_ge(sem("dve_step"), dve.next("dve_step"))
                        if n < TOPK // 8 - 1:
                            eng.match_replace(w[:, 0:ns], m8, src[:, 0:ns], TAKEN).then_inc(sem("dve_step"), 1)
                            eng.wait_ge(sem("dve_step"), dve.next("dve_step"))
                            src = w
                    least = m8[:, 7:8]
                    sel = selbias[:, i, 0:ns]
                    ts_(sel, a[:, 0:ns], least, 0.0, ALU.is_gt, ALU.add, accum_out=cnt).then_inc(sem("dve_step"), 1)
                    eng.wait_ge(sem("dve_step"), dve.next("dve_step"))
                    ts_(a[:, 0:ns], a[:, 0:ns], least, None, ALU.is_equal).then_inc(sem("dve_step"), 1)
                    eng.wait_ge(sem("dve_step"), dve.next("dve_step"))
                    ts_(need, cnt, -1.0, float(TOPK), ALU.mult, ALU.add).then_inc(sem("dve_step"), 1)
                    eng.wait_ge(sem("dve_step"), dve.next("dve_step"))
                    eng.tensor_tensor_scan(w[:, 0:ns], a[:, 0:ns], a[:, 0:ns], 0.0, ALU.add, ALU.max).then_inc(sem("dve_step"), 1)
                    eng.wait_ge(sem("dve_step"), dve.next("dve_step"))
                    stt_(w[:, 0:ns], w[:, 0:ns], need, a[:, 0:ns], ALU.is_le, ALU.mult).then_inc(sem("dve_step"), 1)
                    eng.wait_ge(sem("dve_step"), dve.next("dve_step"))
                    tt_(sel, sel, w[:, 0:ns], ALU.add).then_inc(sem("dve_step"), 1)
                    eng.wait_ge(sem("dve_step"), dve.next("dve_step"))
                    ts_(sel, sel, BIG, -BIG, ALU.mult, ALU.add).then_inc(sem("dve_step"), 1)
                    eng.wait_ge(sem("dve_step"), dve.next("dve_step"))
                    tt_(selbias[:, i, dg], selbias[:, i, dg], C("tri_bias"), ALU.add).then_inc(sem("dve_step"), 1)
                    eng.wait_ge(sem("dve_step"), dve.next("dve_step"))

            def attention(jobs):
                def scores(j):
                    job, ns = jobs[j], jobs[j]["ns"]
                    p, c = probs[:, j % 2, 0:ns], slice(j % 2, j % 2 + 1)
                    eng.wait_ge(sem("score_mm"), dve.next("score_mm"))
                    if dve.reused("pT_mm", 2):
                        eng.wait_ge(sem("pT_mm"), dve.freed("pT_mm", 2))
                    stt_(p, PB[6 + j % 2][:, 0:ns], job["scale"], job["bias"], ALU.mult, ALU.add).then_inc(sem("sm_read"), 1)
                    eng.wait_ge(sem("sm_read"), dve.next("sm_read"))
                    eng.reduce_max(mx[:, c], p, axis=AX.X).then_inc(sem("dve_step"), 1)
                    eng.wait_ge(sem("dve_step"), dve.next("dve_step"))
                    ts_(nmx[:, c], mx[:, c], -1.0, None, ALU.mult).then_inc(sem("sm_ready"), 1)
                    eng.wait_ge(sem("sm_ready"), dve.next("sm_ready"))

                def weights(j):
                    p, c = probs[:, j % 2, 0:jobs[j]["ns"]], slice(j % 2, j % 2 + 1)
                    eng.wait_ge(sem("exp_ready"), dve.next("exp_ready"))
                    eng.reciprocal(rden[:, c], den[:, c]).then_inc(sem("dve_step"), 1)
                    eng.wait_ge(sem("dve_step"), dve.next("dve_step"))
                    ts_(p, p, rden[:, c], None, ALU.mult).then_inc(sem("p_ready"), 1)
                    eng.wait_ge(sem("p_ready"), dve.next("p_ready"))

                scores(0)
                for j in range(len(jobs)):
                    if j + 1 < len(jobs):
                        scores(j + 1)
                    weights(j)

            def group_norm(y, dst, eps):
                eng.wait_ge(sem("gn_sum"), dve.next("gn_sum"))
                for b in range(2):
                    ins = stt_(dst[:, 2 * b:2 * b + 2, :].rearrange("p a b -> p (a b)"), PB[4 + b][:, :], -1.0 / 64,
                               y[:, 2 * b:2 * b + 2, :].rearrange("p a b -> p (a b)"), ALU.mult, ALU.add)
                ins.then_inc(sem("dve_step"), 1)
                eng.wait_ge(sem("dve_step"), dve.next("dve_step"))
                tt_(gn_sq, dst, dst, ALU.mult).then_inc(sem("gn_sq"), 1)
                eng.wait_ge(sem("gn_sq"), dve.next("gn_sq"))
                eng.wait_ge(sem("gn_var"), dve.next("gn_var"))
                for b in range(2):
                    ins = ts_(gn_rs[:, 2 * b:2 * b + 2, :].rearrange("p a b -> p (a b)"), PB[6 + b][:, :], 1.0 / 64, eps,
                              ALU.mult, ALU.add)
                ins.then_inc(sem("dve_step"), 1)
                eng.wait_ge(sem("dve_step"), dve.next("dve_step"))
                root(gn_rs)
                tt_(dst, dst, gn_rs, ALU.mult).then_inc(sem("dve_step"), 1)
                eng.wait_ge(sem("dve_step"), dve.next("dve_step"))

            def retention(l):
                eng.wait_ge(sem("decay_in"), 16 * (l + 1))
                for h in range(8):
                    eng.wait_ge(sem("ret_mm"), dve.next("ret_mm"))
                    if dve.reused("ret_out_mm", 2):
                        eng.wait_ge(sem("ret_out_mm"), dve.freed("ret_out_mm", 2))
                    tt_(ret_s[:, h % 2, :], PB[6 + h % 2][:, 0:384], decay_t[:, h, :], ALU.mult).then_inc(sem("ret_s"), 1)
                    eng.wait_ge(sem("ret_s"), dve.next("ret_s"))
                eng.wait_ge(sem("modT_mm"), l + 1)
                rows = VEC2[f"mod_b{l}"][0]
                tt_(mod[:, l, :], PB[3][:, P:P + MOD], vec[:, 2, rows:rows + MOD], ALU.add).then_inc(sem("dve_step"), 1)
                eng.wait_ge(sem("dve_step"), dve.next("dve_step"))
                group_norm(oD, oD, 1e-6)
                for j in range(4):
                    ins = stt_(oD[:, j, :], oD[:, j, :], vcol(l, VEC1, "ret_gn_g", j), rg_t[:, j, :], ALU.mult, ALU.mult)
                ins.then_inc(sem("oD_ready"), 1)
                eng.wait_ge(sem("oD_ready"), dve.next("oD_ready"))

            def inverse(blocks):
                for n in range(5):
                    for g in range(blocks // 4):
                        eng.wait_ge(sem("sq_mm"), dve.next("sq_mm"))
                        eng.tensor_copy(MT[:, 4 * g:4 * g + 4, :].rearrange("p a b -> p (a b)"),
                                        PB[4 * g + 1][:, :]).then_inc(sem("sqT_ev"), 1)
                        eng.wait_ge(sem("sqT_ev"), dve.next("sqT_ev"))
                    for g in range(blocks // 4):
                        eng.wait_ge(sem("inv_mm"), dve.next("inv_mm"))
                        v = INV[:, 4 * g:4 * g + 4, :].rearrange("p a b -> p (a b)")
                        tt_(v, v, PB[4 * g + 2][:, :], ALU.add).then_inc(sem("inv_add"), 1)
                        eng.wait_ge(sem("inv_add"), dve.next("inv_add"))

            def head_sums(names, dst, other):
                for b in range(2):
                    ins = tt_(dst[:, 2 * b:2 * b + 2, :], PB[names + b][:, :].rearrange("p (a b) -> p a b", b=S),
                              other[:, 2 * b:2 * b + 2, :], ALU.mult)
                return ins

            def rwkv(l):
                eng.wait_ge(sem("shifted"), dve.next("shifted", len(SHIFTED)))
                r_s, k_s, v_s = shifted["r"], shifted["k"], shifted["v"]
                for j in range(4):
                    ins = ts_(KK[:, j, :], k_s[:, j, :], vcol(l, VEC1, "rwkv_k_k", j), None, ALU.mult)
                ins.then_inc(sem("dve_step"), 1)
                eng.wait_ge(sem("dve_step"), dve.next("dve_step"))
                tt_(RL, KK, KK, ALU.mult).then_inc(sem("kk_sq"), 1)
                eng.wait_ge(sem("kk_sq"), dve.next("kk_sq"))
                eng.wait_ge(sem("kk_root"), dve.next("kk_root"))
                ts_(EX, EX, 1e-12, None, ALU.max).then_inc(sem("dve_step"), 1)
                eng.wait_ge(sem("dve_step"), dve.next("dve_step"))
                eng.reciprocal(EX, EX).then_inc(sem("dve_step"), 1)
                eng.wait_ge(sem("dve_step"), dve.next("dve_step"))
                tt_(KK, KK, EX, ALU.mult).then_inc(sem("dve_step"), 1)
                eng.wait_ge(sem("dve_step"), dve.next("dve_step"))
                copied_out(("w2", l, 3))
                ts_(LD, LD, -float(np.exp(-0.5)), None, ALU.mult).then_inc(sem("dve_step"), 1)
                eng.wait_ge(sem("dve_step"), dve.next("dve_step"))
                for j in range(4):
                    for c in range(S // CH):
                        q = slice(CH * c, CH * c + CH)
                        ins = eng.tensor_tensor_scan(RL[:, j, q], LD[:, j, q], LD[:, j, q], 0.0, ALU.add, ALU.min)
                ins.then_inc(sem("dve_step"), 1)
                eng.wait_ge(sem("dve_step"), dve.next("dve_step"))
                tt_(EX, RL, LD, ALU.subtract).then_inc(sem("log_decays"), 1)
                eng.wait_ge(sem("log_decays"), dve.next("log_decays"))
                copied_out(("a2", l, 3))
                for j in range(4):
                    ins = ts_(LD[:, j, :], RA[:, j, :], 1.0, vcol(l, VEC1, "rwkv_k_a", j), ALU.subtract, ALU.mult)
                ins.then_inc(sem("dve_step"), 1)
                eng.wait_ge(sem("dve_step"), dve.next("dve_step"))
                for j in range(4):
                    ins = stt_(k_s[:, j, :], LD[:, j, :], 1.0, k_s[:, j, :], ALU.add, ALU.mult)
                ins.then_inc(sem("dve_step"), 1)
                eng.wait_ge(sem("dve_step"), dve.next("dve_step"))
                tt_(RA, KK, RA, ALU.mult).then_inc(sem("dve_step"), 1)
                eng.wait_ge(sem("dve_step"), dve.next("dve_step"))
                for j in range(4):
                    ins = stt_(LD[:, j, :], r_s[:, j, :], vcol(l, VEC1, "rwkv_r_k", j), k_s[:, j, :], ALU.mult, ALU.mult)
                ins.then_inc(sem("bonus_in"), 1)
                eng.wait_ge(sem("bonus_in"), dve.next("bonus_in"))
                eng.wait_ge(sem("bonus_sum"), dve.next("bonus_sum"))
                head_sums(6, LD, v_s).then_inc(sem("dve_step"), 1)
                eng.wait_ge(sem("dve_step"), dve.next("dve_step"))
                eng.memset(arena[:, W0:W0 + 5120], 0.0)
                eng.memset(ST, 0.0).then_inc(sem("state_up"), 1)
                eng.wait_ge(sem("state_up"), dve.next("state_up"))
                eng.wait_ge(sem("decays"), dve.next("decays"))
                for half in range(2):
                    def part(x, r):
                        return x[r, :, P * half:P * half + P].rearrange("p t (c n) -> p t c n", c=2)

                    for s in range(2):
                        r, q = slice(CH * s, CH * s + CH), slice(CH * s, CH * s + CH)

                        def place(x):
                            return x[r, :, q].rearrange("p (t c) n -> p t c n", c=2)

                        tt_(place(KR[:, :, 0, :]), part(KK, r), part(EX, r), ALU.mult)
                        tt_(place(KR[:, :, 1, :]), part(r_s, r), part(EP, r), ALU.mult)
                        tt_(place(BMb), part(RA, r), part(EN, r), ALU.mult)
                        tt_(place(KMb), part(k_s, r), part(EN, r), ALU.mult)
                        ins = eng.tensor_copy(place(VD), part(v_s, r))
                    ins.then_inc(sem("blocks_ready"), 1)
                    eng.wait_ge(sem("blocks_ready"), dve.next("blocks_ready"))
                    for b in range(8):
                        p0 = 4 * (b % 2)
                        eng.wait_ge(sem("block_mm"), dve.next("block_mm"))
                        tt_(MS[:, b, :], PB[p0][:, 0:P], C("mask_neg")[:, 0:P], ALU.mult)
                        tt_(ARb[:, b, :], PB[p0][:, P:S], C("mask_neg")[:, P:S], ALU.mult)
                        tt_(KK2[:, b, :, :].rearrange("p a b -> p (a b)"), PB[p0 + 1][:, 0:S], C("mask_pos"), ALU.mult)
                        tt_(MT[:, b, :], PB[p0 + 2][:, 0:P], C("mask_low_neg"), ALU.mult).then_inc(sem("dve_step"), 1)
                        eng.wait_ge(sem("dve_step"), dve.next("dve_step"))
                        tt_(INV[:, b, :], MS[:, b, :], C("ident"), ALU.add).then_inc(sem("block_ev"), 1)
                        eng.wait_ge(sem("block_ev"), dve.next("block_ev"))
                    inverse(8)
                    for c in range(2):
                        eng.wait_ge(sem("rhs_mm"), dve.next("rhs_mm"))
                        ts_(RHS.rearrange("p a b -> p (a b)"), PB[0][:, :], -1.0, None, ALU.mult).then_inc(sem("rhs_ev"), 1)
                        eng.wait_ge(sem("rhs_ev"), dve.next("rhs_ev"))
                        if half == 1 and c == 1:
                            break
                        eng.wait_ge(sem("state_mm"), dve.next("state_mm"))
                        tt_(STMP.rearrange("p a b -> p (a b)"), ST.rearrange("p a b -> p (a b)"), PB[3][:, :], ALU.add).then_inc(sem("dve_step"), 1)
                        eng.wait_ge(sem("dve_step"), dve.next("dve_step"))
                        t = CH * (2 * half + c) + CH - 1
                        for p in range(4):
                            ins = ts_(ST[:, p, :], STMP[:, p, :], EP[:, p, t:t + 1], None, ALU.mult)
                        ins.then_inc(sem("state_up"), 1)
                        eng.wait_ge(sem("state_up"), dve.next("state_up"))
                dve.seen["state_mm"] += 1
                group_norm(YT, oB, 64e-5)
                for j in range(4):
                    ins = ts_(oB[:, j, :], oB[:, j, :], vcol(l, VEC1, "rwkv_ln_g", j), vcol(l, VEC1, "rwkv_ln_b", j),
                              ALU.mult, ALU.add)
                ins.then_inc(sem("dve_step"), 1)
                eng.wait_ge(sem("dve_step"), dve.next("dve_step"))
                tt_(oB, oB, LD, ALU.add).then_inc(sem("dve_step"), 1)
                eng.wait_ge(sem("dve_step"), dve.next("dve_step"))
                copied_out(("g2", l, 3))
                tt_(oB, oB, RG, ALU.mult).then_inc(sem("oB_ready"), 1)
                eng.wait_ge(sem("oB_ready"), dve.next("oB_ready"))

            def merge(l):
                for m in range(KD):
                    for b in range(4):
                        copied_out(("branch", l, m, b))
                        dst = prod_s[:, 0, :] if b else merged[:, m, :]
                        tt_(dst, gate_s[:, b, :], proj_s[:, b, :], ALU.mult).then_inc(sem("gated"), 1)
                        eng.wait_ge(sem("gated"), dve.next("gated"))
                        if b:
                            ins = tt_(merged[:, m, :], merged[:, m, :], dst, ALU.add)
                            if (m, b) != (KD - 1, 3):
                                ins.then_inc(sem("dve_step"), 1)
                                eng.wait_ge(sem("dve_step"), dve.next("dve_step"))
                ins.then_inc(sem("merged"), 1)
                eng.wait_ge(sem("merged"), dve.next("merged"))

            def residual(name, l, buf, gain=None):
                for m in range(KD):
                    copied_out((name, l, m))
                    if gain is None:
                        ins = tt_(xT[:, m, :], xT[:, m, :], buf[:, m % 4, :], ALU.add)
                    else:
                        ins = stt_(xT[:, m, :], buf[:, m % 4, :], gain[:, m:m + 1], xT[:, m, :], ALU.mult, ALU.add)
                    ins.then_inc(sem("res_add"), 1)
                    eng.wait_ge(sem("res_add"), dve.next("res_add"))

            def gdn():
                for j in range(12):
                    copied_out(("conv", j))
                    for i in range(4):
                        w = vcol(3, VEC3, "conv", 12 * i + j)
                        x = conv_in[:, j, i:i + S]
                        if i == 0:
                            ts_(gqkv[:, j, :], x, w, None, ALU.mult).then_inc(sem("dve_step"), 1)
                            eng.wait_ge(sem("dve_step"), dve.next("dve_step"))
                        else:
                            ins = stt_(gqkv[:, j, :], x, w, gqkv[:, j, :], ALU.mult, ALU.add)
                            if i < 3:
                                ins.then_inc(sem("dve_step"), 1)
                                eng.wait_ge(sem("dve_step"), dve.next("dve_step"))
                    ins.then_inc(sem("conv_done"), 1)
                    eng.wait_ge(sem("conv_done"), dve.next("conv_done"))
                copied_out(("ba",))
                eng.wait_ge(sem("ab_in"), 32)
                for t in range(TT):
                    ins = tt_(sp_t[:, 0, t, :], ba_t[:, t, 4:8], ab_t[:, 0, 4:8], ALU.add)
                ins.then_inc(sem("dve_step"), 1)
                eng.wait_ge(sem("dve_step"), dve.next("dve_step"))
                stt_(sp_t[:, 1, :, :], sp_t[:, 0, :, :], -1.0, sp_t[:, 0, :, :], ALU.mult, ALU.max).then_inc(sem("dve_step"), 1)
                eng.wait_ge(sem("dve_step"), dve.next("dve_step"))
                ts_(sp_t[:, 2, :, :], sp_t[:, 0, :, :], 0.0, None, ALU.max).then_inc(sem("sp_x"), 1)
                eng.wait_ge(sem("sp_x"), dve.next("sp_x"))
                eng.wait_ge(sem("sp_ln"), dve.next("sp_ln"))
                tt_(sp_t[:, 2, :, :], sp_t[:, 2, :, :], sp_t[:, 1, :, :], ALU.add).then_inc(sem("dve_step"), 1)
                eng.wait_ge(sem("dve_step"), dve.next("dve_step"))
                for t in range(TT):
                    ins = stt_(glog[:, t, :], sp_t[:, 2, t, :], -1.0, ab_t[:, 0, 0:4], ALU.mult, ALU.mult)
                ins.then_inc(sem("dve_step"), 1)
                eng.wait_ge(sem("dve_step"), dve.next("dve_step"))
                eng.wait_ge(sem("l2_mm"), dve.next("l2_mm"))
                for b in range(4):
                    ins = ts_(gsq[:, 2 * b:2 * b + 2, :].rearrange("p a b -> p (a b)"), PB[4 + b][:, :], 1e-6, None, ALU.add)
                ins.then_inc(sem("dve_step"), 1)
                eng.wait_ge(sem("dve_step"), dve.next("dve_step"))
                root(gsq)
                stt_(gq, gsq[:, 0:4, :], P ** -0.5, gq, ALU.mult, ALU.mult).then_inc(sem("dve_step"), 1)
                eng.wait_ge(sem("dve_step"), dve.next("dve_step"))
                tt_(gk, gsq[:, 4:8, :], gk, ALU.mult).then_inc(sem("dve_step"), 1)
                eng.wait_ge(sem("dve_step"), dve.next("dve_step"))
                eng.tensor_copy(small[:, 41:42], small[:, 41:42]).then_inc(sem("gdn_gate"), 1)
                eng.wait_ge(sem("gdn_gate"), dve.next("gdn_gate"))
                eng.wait_ge(sem("gcum_mm"), dve.next("gcum_mm"))
                eng.tensor_copy(gl_t.rearrange("p a b -> p (a b)"), PB[4][:, 0:16]).then_inc(sem("dve_step"), 1)
                eng.wait_ge(sem("dve_step"), dve.next("dve_step"))
                eng.tensor_copy(eg_t[:, 0, :, :], gl_t[:, :, 0:4]).then_inc(sem("dve_step"), 1)
                eng.wait_ge(sem("dve_step"), dve.next("dve_step"))
                tt_(eg_t[:, 1, :, :], gl_t[:, :, 4:8], gl_t[:, :, 0:4], ALU.subtract).then_inc(sem("gdn_cum"), 1)
                eng.wait_ge(sem("gdn_cum"), dve.next("gdn_cum"))
                for b in range(8):
                    ins = ts_(gcols[:, b, :], C("ones"), gl_t[:, b % 2, b // 2:b // 2 + 1], None, ALU.mult)
                ins.then_inc(sem("decay_rows"), 1)
                eng.wait_ge(sem("decay_rows"), dve.next("decay_rows"))
                eng.wait_ge(sem("erow_ready"), dve.next("erow_ready"))
                for b in range(8):
                    ins = stt_(dmat[:, b, :], PB[6 + b // 4][:, (b % 4) * P:(b % 4) * P + P],
                               gl_t[:, b % 2, b // 2:b // 2 + 1], C("chunk_low_bias"), ALU.subtract, ALU.subtract)
                ins.then_inc(sem("dmat_in"), 1)
                eng.wait_ge(sem("dmat_in"), dve.next("dmat_in"))
                eng.tensor_copy(small[:, 42:43], small[:, 42:43]).then_inc(sem("gdn_qk"), 1)
                eng.wait_ge(sem("gdn_qk"), dve.next("gdn_qk"))
                eng.wait_ge(sem("eg_ready"), dve.next("eg_ready"))
                tt_(eg_t[:, 0, :, :], eg_t[:, 0, :, :], beta_t, ALU.mult).then_inc(sem("dve_step"), 1)
                eng.wait_ge(sem("dve_step"), dve.next("dve_step"))
                eng.wait_ge(sem("dmat_ready"), dve.next("dmat_ready"))
                for b in range(8):
                    ps, h, t = PB[4 + b % 2], b // 2, b % 2
                    beta = beta_t[:, t, h:h + 1]
                    eng.wait_ge(sem("gdn_mm"), dve.next("gdn_mm"))
                    tt_(MT[:, b, :], ps[:, 0:P], dmat[:, b, :], ALU.mult).then_inc(sem("dve_step"), 1)
                    eng.wait_ge(sem("dve_step"), dve.next("dve_step"))
                    tt_(qk_t[:, b, :], ps[:, P:S], dmat[:, b, :], ALU.mult)
                    stt_(MT[:, b, :], MT[:, b, :], beta, C("mask_low_neg"), ALU.mult, ALU.mult).then_inc(sem("gdn_l"), 1)
                    eng.wait_ge(sem("gdn_l"), dve.next("gdn_l"))
                    ts_(kb_t[:, b, :], ps[:, S:384], eg_t[:, 0, t, h:h + 1], None, ALU.mult)
                    ts_(kd_t[:, b, :], ps[:, S:384], eg_t[:, 1, t, h:h + 1], None, ALU.mult)
                    ts_(vb_t[:, b, :], ps[:, 384:512], beta, None, ALU.mult).then_inc(sem("gdn_tok"), 1)
                    eng.wait_ge(sem("gdn_tok"), dve.next("gdn_tok"))
                for b in range(8):
                    ps = PB[b % 4]
                    eng.wait_ge(sem("gdn_tr_mm"), dve.next("gdn_tr_mm"))
                    eng.tensor_copy(MS[:, b, :], ps[:, 0:P])
                    eng.tensor_copy(qk2_t[:, b, :], ps[:, P:S])
                    tt_(INV[:, b, :], ps[:, 0:P], C("ident"), ALU.add).then_inc(sem("gdn_tr"), 1)
                    eng.wait_ge(sem("gdn_tr"), dve.next("gdn_tr"))
                inverse(8)
                tt_(gq, gq, erow, ALU.mult)
                eng.memset(vn_t, 0.0)
                eng.memset(GS, 0.0).then_inc(sem("gstate_up"), 1)
                eng.wait_ge(sem("gstate_up"), dve.next("gstate_up"))
                for c in range(4):
                    t, r = c // 2, slice(CH * (c % 2), CH * (c % 2) + CH)
                    eng.wait_ge(sem("gv_mm"), dve.next("gv_mm"))
                    u = uw_t[r, :, 0:P].rearrange("p (h t) v -> p h t v", t=2)[:, :, t, :]
                    tt_(vn_t[r], u, PB[0][r, :].rearrange("p (a b) -> p a b", b=P), ALU.subtract).then_inc(sem("gv_ev"), 1)
                    eng.wait_ge(sem("gv_ev"), dve.next("gv_ev"))
                    if c == 3:
                        break
                    eng.wait_ge(sem("gstate_mm"), dve.next("gstate_mm"))
                    for h in range(4):
                        ins = stt_(GS[:, h, :], GS[:, h, :], erow[:, h, CH * c + CH - 1:CH * c + CH],
                                   PB[2][:, h * P:h * P + P], ALU.mult, ALU.add)
                    ins.then_inc(sem("gstate_up"), 1)
                    eng.wait_ge(sem("gstate_up"), dve.next("gstate_up"))
                eng.wait_ge(sem("go_mm"), dve.next("go_mm"))
                for b in range(2):
                    ins = ts_(gsq[:, 2 * b:2 * b + 2, :].rearrange("p a b -> p (a b)"), PB[4 + b][:, :], 1.0 / P, 1e-6,
                              ALU.mult, ALU.add)
                ins.then_inc(sem("dve_step"), 1)
                eng.wait_ge(sem("dve_step"), dve.next("dve_step"))
                root(gsq[:, 0:4, :])
                stt_(mix_t[:, 0:4, :], mix_t[:, 0:4, :], vcol(3, VEC3, "gdn_o_norm"), gsq[:, 0:4, :],
                          ALU.mult, ALU.mult).then_inc(sem("dve_step"), 1)
                eng.wait_ge(sem("dve_step"), dve.next("dve_step"))
                copied_out(("z", 3))
                tt_(mix_t[:, 0:4, :], mix_t[:, 0:4, :], z_t, ALU.mult).then_inc(sem("gdn_ready"), 1)
                eng.wait_ge(sem("gdn_ready"), dve.next("gdn_ready"))

            def latent_norms():
                copied_out(("c", 5))
                for first, n, name in ((0, 4, "mla_q_norm"), (4, 2, "mla_kv_norm")):
                    inv_norm(n * P, 1e-6)
                    for k in range(n):
                        ins = stt_(lat[:, first + k, :], lat[:, first + k, :], vcol(3, VEC3, name, k), rstd,
                                   ALU.mult, ALU.mult)
                    ins.then_inc(sem("dve_step"), 1)
                    eng.wait_ge(sem("dve_step"), dve.next("dve_step"))
                eng.tensor_copy(small[:, 43:44], small[:, 43:44]).then_inc(sem("lat_ready"), 1)
                eng.wait_ge(sem("lat_ready"), dve.next("lat_ready"))

            def top16(values, index, src, spare):
                eng.max(values[:, 0:8], src).then_inc(sem("dve_step"), 1)
                eng.wait_ge(sem("dve_step"), dve.next("dve_step"))
                eng.max_index(index[:, 0:8], values[:, 0:8], src)
                eng.match_replace(spare, values[:, 0:8], src, TAKEN).then_inc(sem("dve_step"), 1)
                eng.wait_ge(sem("dve_step"), dve.next("dve_step"))
                eng.max(values[:, 8:16], spare).then_inc(sem("dve_step"), 1)
                eng.wait_ge(sem("dve_step"), dve.next("dve_step"))
                eng.max_index(index[:, 8:16], values[:, 8:16], spare).then_inc(sem("dve_step"), 1)
                eng.wait_ge(sem("dve_step"), dve.next("dve_step"))

            def router(l):
                for t in range(TT):
                    eng.wait_ge(sem("key_ev"), dve.next("key_ev", 4))
                    for c in range(16):
                        top16(tv[:, c, :], ti[:, c, :], key_t[:, t, c, :], key_s[:, c % 2, :])
                    eng.tensor_copy(tif, ti).then_inc(sem("dve_step"), 1)
                    eng.wait_ge(sem("dve_step"), dve.next("dve_step"))
                    half = [x.rearrange("p (h s) k -> p h s k", s=2) for x in (tv, tif)]
                    wide = [P, 8, 16, 16]

                    def square4(x):
                        return x.rearrange("p h (a b) -> p h a b", b=16)

                    for h in range(8):
                        ins = tt_(cand[:, h, :].rearrange("p (a b) -> p a b", b=16),
                                  half[0][:, h, 0, :].unsqueeze(2).to_broadcast([P, 16, 16]),
                                  half[0][:, h, 1, :].unsqueeze(1).to_broadcast([P, 16, 16]), ALU.add)
                    ins.then_inc(sem("dve_step"), 1)
                    eng.wait_ge(sem("dve_step"), dve.next("dve_step"))
                    for h in range(8):
                        top16(cv[:, t, h, :], ci[:, h, :], cand[:, h, :], cand_s[:, h % 2, :])
                    ts_(ci_row, ci, 4, None, ALU.logical_shift_right).then_inc(sem("dve_step"), 1)
                    eng.wait_ge(sem("dve_step"), dve.next("dve_step"))
                    ts_(ci, ci, 15, None, ALU.bitwise_and).then_inc(sem("dve_step"), 1)
                    eng.wait_ge(sem("dve_step"), dve.next("dve_step"))
                    eng.tensor_copy(first_k, ci_row)
                    eng.tensor_copy(second, ci).then_inc(sem("dve_step"), 1)
                    eng.wait_ge(sem("dve_step"), dve.next("dve_step"))
                    for i, pos in enumerate((first_k, second)):
                        for h in range(8):
                            ins = tt_(hot[:, h, :].rearrange("p (a b) -> p a b", b=16),
                                      pos[:, h, :].unsqueeze(2).to_broadcast([P, 16, 16]),
                                      C("iota")[:, 0:16].unsqueeze(1).to_broadcast([P, 16, 16]), ALU.is_equal)
                        ins.then_inc(sem("dve_step"), 1)
                        eng.wait_ge(sem("dve_step"), dve.next("dve_step"))
                        for h in range(8):
                            ins = tt_(hot[:, h, :].rearrange("p (a b) -> p a b", b=16),
                                      hot[:, h, :].rearrange("p (a b) -> p a b", b=16),
                                      half[1][:, h, i, :].unsqueeze(1).to_broadcast([P, 16, 16]), ALU.mult)
                        ins.then_inc(sem("dve_step"), 1)
                        eng.wait_ge(sem("dve_step"), dve.next("dve_step"))
                        eng.reduce_sum(pick_t[:, i, t, :], hot.rearrange("p h (a b) -> p (h a) b", b=16), axis=AX.X).then_inc(sem("dve_step"), 1)
                        eng.wait_ge(sem("dve_step"), dve.next("dve_step"))
                for t in range(TT):
                    eng.tensor_copy(esum[:, 0, t, :].unsqueeze(2), cv[:, t, :, 0:1]).then_inc(sem("dve_step"), 1)
                    eng.wait_ge(sem("dve_step"), dve.next("dve_step"))
                    tt_(cv[:, t, :, :], cv[:, t, :, :], esum[:, 0, t, :].unsqueeze(2).to_broadcast([P, 8, 16]),
                             ALU.subtract).then_inc(sem("dve_step"), 1)
                    eng.wait_ge(sem("dve_step"), dve.next("dve_step"))
                eng.tensor_copy(small[:, 44:45], small[:, 44:45]).then_inc(sem("gate_logits"), 1)
                eng.wait_ge(sem("gate_logits"), dve.next("gate_logits"))
                eng.wait_ge(sem("gate_exp"), dve.next("gate_exp"))
                for t in range(TT):
                    eng.reduce_sum(esum[:, 0, t, :], cv[:, t, :, :], axis=AX.X).then_inc(sem("dve_step"), 1)
                    eng.wait_ge(sem("dve_step"), dve.next("dve_step"))
                    eng.reciprocal(esum[:, 1, t, :], esum[:, 0, t, :]).then_inc(sem("dve_step"), 1)
                    eng.wait_ge(sem("dve_step"), dve.next("dve_step"))
                    tt_(pick_t[:, 2, t, :].rearrange("p (a b) -> p a b", b=16), cv[:, t, :, :],
                             esum[:, 1, t, :].unsqueeze(2).to_broadcast([P, 8, 16]), ALU.mult).then_inc(sem("dve_step"), 1)
                    eng.wait_ge(sem("dve_step"), dve.next("dve_step"))
                eng.tensor_copy(small[:, 45:46], small[:, 45:46]).then_inc(sem("picked"), 1)
                eng.wait_ge(sem("picked"), dve.next("picked"))

            def gate_rows(l):
                base = 64 * l

                def group(n, b):
                    for j in range(4):
                        t = n * 4 + j
                        at = slice(t, t + 1) if isinstance(t, int) else bass.ds(t, 1)
                        ts_(one_d[:, b, j, :], C("iota"), selT[:, 0, at], selT[:, 2, at], ALU.is_equal, ALU.mult)
                        ins = ts_(one_p[:, b, j, :], C("iota"), selT[:, 1, at], None, ALU.is_equal)
                    ins.then_inc(sem("one_rows"), 1)

                eng.wait_ge(sem("pickT_ev"), dve.next("pickT_ev"))
                for b in range(2):
                    group(b, b)
                with eng.Fori(1, 32) as i:
                    for b in range(2):
                        if positive(i * 2 + (b - 1 + base)):
                            eng.wait_ge(sem("one_rows"), i * 2 + (b - 1 + base))
                        if positive(i * 2 + (b - 1 + base)):
                            eng.wait_ge(sem("gate_mm"), i * 2 + (b - 1 + base))
                        group(i * 2 + b, b)

            def expert_tiles(l):
                base = NKEY * l

                def u_low(e):
                    for q in range(2):
                        d = slice(q * 512, q * 512 + 512)
                        eng.wait_ge(sem("uH_ready"), e * 2 + (2 * base + q + 1))
                        tt_(u_parts[:, 1, d], PB[4 + q][:, :], u_parts[:, 0, d].bitcast(F32), ALU.subtract).then_inc(sem("uL_ready"), 1)

                def weigh(e, j):
                    b = j % 2
                    eng.wait_ge(sem("gelu_done"), e + (1 + base))
                    col = slice(e, e + 1) if isinstance(e, int) else bass.ds(e, 1)
                    w = gelu[:, b, :]
                    tt_(w.unsqueeze(2), w.unsqueeze(2), gates[:, :, col], ALU.mult).then_inc(sem("weighed"), 1)
                    eng.wait_ge(sem("wH_ready"), e + (1 + base))
                    tt_(w_low[:, b, :], w, w_high[:, b, :].bitcast(F32), ALU.subtract).then_inc(sem("wL_ready"), 1)
                    eng.wait_ge(sem("vH_ready"), e + (1 + base))
                    tt_(v_low[:, j, :], ring[:, 2 + j, :], v_high.bitcast(F32), ALU.subtract).then_inc(sem("vL_ready"), 1)

                eng.wait_ge(sem("hH_ready"), l + 1)
                tt_(h_low, hT, h_high.bitcast(F32), ALU.subtract).then_inc(sem("h_split"), 1)
                eng.wait_ge(sem("gate_ev"), 64 * (l + 1))
                u_low(0)
                for e in range(4):
                    u_low(e + 1)
                    weigh(e, e)
                with eng.Fori(1, 31) as i:
                    for j in range(4):
                        u_low(i * 4 + (j + 1))
                        weigh(i * 4 + j, j)
                for j in range(4):
                    if j < 3:
                        u_low(125 + j)
                    weigh(124 + j, j)
                eng.wait_ge(sem("v_free"), base + NKEY)
                for q in range(2):
                    ins = eng.tensor_copy(moe_t[:, 1, q * 512:q * 512 + 512], PB[2 + q][:, :])
                ins.then_inc(sem("experts1_ev"), 1)
                eng.wait_ge(sem("moe_mm"), dve.next("moe_mm"))
                for k in range(KD):
                    ins = stt_(xT[:, k, :], PB[4 + k // 2][:, (k % 2) * S:(k % 2) * S + S], mod[:, l, 40 + k:41 + k],
                               xT[:, k, :], ALU.mult, ALU.add)
                ins.then_inc(sem("x_ready"), 1)
                eng.wait_ge(sem("x_ready"), dve.next("x_ready"))

            eng.memset(rows_in, 0.0).then_inc(sem("rows_zero"), 1)
            eng.wait_ge(sem("rows_zero"), dve.next("rows_zero"))
            eng.wait_ge(sem("setup_in"), 16 * SETUP)
            eng.memset(small[:, :], 0.0)
            eng.tensor_copy(wT[:, :, :], ipos).then_inc(sem("dve_step"), 1)
            eng.wait_ge(sem("dve_step"), dve.next("dve_step"))
            angles(0, "att", 0, 0)
            angles(1, "ret", 1, 0)
            for i in range(2):
                cosine(i)
            eng.wait_ge(sem("vec_ready"), 1)
            eng.wait_ge(sem("x_ready"), dve.next("x_ready"))
            for l in range(DEPTH):
                norm(hT, vec[:, l, 0:8]).then_inc(sem("h_ready"), 1)
                eng.wait_ge(sem("h_ready"), dve.next("h_ready"))
                rope(att_rope(l), 0)
                rope(ret_rope(l), 1)
                indexer(l)
                attention(dsa_jobs())
                retention(l)
                rwkv(l)
                merge(l)
                residual("wout", l, res_s)
                norm(hT, vec[:, l, 8:16]).then_inc(sem("h_ready"), 1)
                eng.wait_ge(sem("h_ready"), dve.next("h_ready"))
                residual("down", l, res_s)
            norm(xT, vec[:, 3, VEC3["final_norm_g"][0]:VEC3["final_norm_g"][0] + 8]).then_inc(sem("x_ready"), 1)
            eng.wait_ge(sem("x_ready"), dve.next("x_ready"))
            angles(0, "moba", 2, 1)
            angles(1, "mla", 3, 1)
            for i in range(2):
                cosine(i)
            for l in range(DEPTH):
                modulated_norm(l, 0)
                if l == 0:
                    eng.memset(conv_in[:, :, 0:3], 0.0).then_inc(sem("dve_step"), 1)
                    eng.wait_ge(sem("dve_step"), dve.next("dve_step"))
                    rope(moba_rope(), 0)
                    gdn()
                    attention(moba_jobs())
                else:
                    latent_norms()
                    rope(mla_rope(), 1)
                    eng.memset(kr2_t, 0.0).then_inc(sem("dve_step"), 1)
                    eng.wait_ge(sem("dve_step"), dve.next("dve_step"))
                    for s in range(2):
                        r = slice(64 * s, 64 * s + 64)
                        ins = eng.tensor_copy(kr2_t[r, s, :], kr_t[r, 0, :])
                    ins.then_inc(sem("kr_ready"), 1)
                    eng.wait_ge(sem("kr_ready"), dve.next("kr_ready"))
                    attention(mla_jobs())
                residual("mix", l, res2_s, mod[:, l, 16:24])
                modulated_norm(l, 1)
                router(l)
                gate_rows(l)
                expert_tiles(l)
            norm(hT, vec[:, 3, VEC3["final_norm_2"][0]:VEC3["final_norm_2"][0] + 8], 1e-6).then_inc(sem("h_ready"), 1)
            eng.wait_ge(sem("h_ready"), dve.next("h_ready"))


def kernel(**inputs):
    import numpy as _np
    import concourse.bacc as _bacc
    from concourse import mybir as _mybir
    from concourse.bass_utils import run_bass_kernel_spmd as _run

    nc = _bacc.Bacc("TRN2", target_bir_lowering=False, num_devices=1)
    arrays, io = {}, {}
    laid_out = {name: _np.ascontiguousarray(a) for name, a in inputs.items()}
    laid_out["consts"] = constants()
    laid_out["decay"] = retention_decay()
    for name, a in laid_out.items():
        arrays[f"in_{name}"] = a
        io[name] = nc.dram_tensor(f"in_{name}", a.shape, _mybir.dt.from_np(a.dtype), kind="ExternalInput").ap()
    out = nc.dram_tensor("out_0", (1, S, D), F32, kind="ExternalOutput").ap()
    two_stacks(nc, io, out)
    return _run(nc, [arrays], core_ids=[0]).results[0]["out_0"]
```
